# Optimizing a Trainium2 kernel written in Bass

```python
import math
import jax, jax.numpy as jnp
from jax import lax
import numpy as np

D_MODEL = 1024
BATCH = 1
SEQ = 512
DEPTH = 2

N_MIXERS = 2
N_SUB = 3
D_FF = 2816
MLSTM_HEADS = 8
MLSTM_DQK = D_MODEL // (2 * MLSTM_HEADS)
MLSTM_DV = D_MODEL // MLSTM_HEADS
MLSTM_CHUNK = 64
CONV_WIDTH = 4
MLSTM_QK_COLS = 2 * MLSTM_HEADS * MLSTM_DQK
MLSTM_V_COLS = MLSTM_HEADS * MLSTM_DV
MLSTM_PROJ = MLSTM_QK_COLS + 2 * MLSTM_V_COLS + 2 * MLSTM_HEADS
DIL_GROUPS = ((128, 1), (512, 4), (2048, 16))
N_GROUPS = len(DIL_GROUPS)
ATTN_HEADS = 8
ATTN_HEAD_DIM = D_MODEL // ATTN_HEADS
ATTN_PROJ = N_GROUPS * 3 * ATTN_HEADS * ATTN_HEAD_DIM
ALPHA = (2 * DEPTH) ** 0.25
BETA = (8 * DEPTH) ** -0.25
LN_EPS = 1e-5
RMS_EPS = 1e-6
N_MLSTM_LAYERS = (DEPTH + 1) // 2
N_ATTN_LAYERS = DEPTH // 2

kernel_name = 'hybrid_mlstm_dilated_attn_macaron_deepnorm_adaln'

def _layer_norm(x, g, b):
    xf = x.astype(jnp.float32)
    mu = xf.mean(-1, keepdims=True)
    var = jnp.square(xf - mu).mean(-1, keepdims=True)
    return ((xf - mu) * lax.rsqrt(var + LN_EPS) * g.astype(jnp.float32) + b.astype(jnp.float32)).astype(x.dtype)

def _swiglu(h, w_in, w_out):
    g, u = jnp.split(h @ w_in, 2, axis=-1)
    return (jax.nn.silu(g) * u) @ w_out

def _causal_dwconv(x, w):
    k_w, ch = w.shape
    xp = jnp.pad(x, ((0, 0), (k_w - 1, 0), (0, 0)))
    return lax.conv_general_dilated(xp, w[:, None, :].astype(x.dtype), window_strides=(1,), padding='VALID',
                                    dimension_numbers=('NWC', 'WIO', 'NWC'), feature_group_count=ch)

def _mlstm_cell_chunkwise(q, k, v, i_pre, log_f):
    B, S, H, DK = q.shape
    DV = v.shape[-1]
    L = MLSTM_CHUNK
    nc = S // L

    def chunks(t):
        return jnp.moveaxis(t.reshape((B, nc, L, H) + t.shape[3:]), 3, 1)

    qc = chunks(q.astype(jnp.float32)) * (DK ** -0.5)
    kc = chunks(k.astype(jnp.float32))
    vc = chunks(v.astype(jnp.float32))
    ig = chunks(i_pre)
    bcum = jnp.cumsum(chunks(log_f), axis=-1)
    b_last = bcum[..., -1]

    a = b_last[..., None] - bcum + ig
    m_loc = a.max(-1)
    wa = jnp.exp(a - m_loc[..., None])
    c_loc = jnp.einsum('bhcl,bhclv,bhclk->bhcvk', wa, vc, kc)
    n_loc = jnp.einsum('bhcl,bhclk->bhck', wa, kc)

    def step(carry, inp):
        c_st, n_st, m_st = carry
        cl, nl, ml, bl = inp
        m_new = jnp.maximum(bl + m_st, ml)
        sp = jnp.exp(bl + m_st - m_new)
        sl = jnp.exp(ml - m_new)
        c_new = sp[..., None, None] * c_st + sl[..., None, None] * cl
        n_new = sp[..., None] * n_st + sl[..., None] * nl
        return (c_new, n_new, m_new), (c_st, n_st, m_st)

    init = (jnp.zeros((B, H, DV, DK), jnp.float32), jnp.zeros((B, H, DK), jnp.float32),
            jnp.zeros((B, H), jnp.float32))
    xs = (jnp.moveaxis(c_loc, 2, 0), jnp.moveaxis(n_loc, 2, 0), jnp.moveaxis(m_loc, 2, 0), jnp.moveaxis(b_last, 2, 0))
    _, (c_prev, n_prev, m_prev) = lax.scan(step, init, xs)
    c_prev = jnp.moveaxis(c_prev, 0, 2)
    n_prev = jnp.moveaxis(n_prev, 0, 2)
    m_prev = jnp.moveaxis(m_prev, 0, 2)

    causal = jnp.tril(jnp.ones((L, L), dtype=bool))
    dlog = jnp.where(causal, bcum[..., :, None] - bcum[..., None, :] + ig[..., None, :], -jnp.inf)
    inter_log = bcum + m_prev[..., None]
    m = jnp.maximum(inter_log, dlog.max(-1))
    sc = jnp.einsum('bhcik,bhcjk->bhcij', qc, kc) * jnp.exp(dlog - m[..., None])
    inter_w = jnp.exp(inter_log - m)
    num = jnp.einsum('bhcij,bhcjv->bhciv', sc, vc) + inter_w[..., None] * jnp.einsum('bhcik,bhcvk->bhciv', qc, c_prev)
    den = sc.sum(-1) + inter_w * jnp.einsum('bhcik,bhck->bhci', qc, n_prev)
    h = num / jnp.maximum(jnp.abs(den), jnp.exp(-m))[..., None]
    return jnp.moveaxis(h, 1, 3).reshape(B, S, H, DV)

def _mlstm_mixer(h, w_in, gate_bias, conv_w, head_gain, w_out):
    B, S, _ = h.shape
    proj = h @ w_in
    qk = proj[..., :MLSTM_QK_COLS]
    v = proj[..., MLSTM_QK_COLS:MLSTM_QK_COLS + MLSTM_V_COLS]
    o = proj[..., MLSTM_QK_COLS + MLSTM_V_COLS:MLSTM_QK_COLS + 2 * MLSTM_V_COLS]
    gates = proj[..., MLSTM_QK_COLS + 2 * MLSTM_V_COLS:].astype(jnp.float32) + gate_bias.astype(jnp.float32)
    qk = jax.nn.silu(_causal_dwconv(qk, conv_w))
    q = qk[..., :MLSTM_QK_COLS // 2].reshape(B, S, MLSTM_HEADS, MLSTM_DQK)
    k = qk[..., MLSTM_QK_COLS // 2:].reshape(B, S, MLSTM_HEADS, MLSTM_DQK)
    v = v.reshape(B, S, MLSTM_HEADS, MLSTM_DV)
    i_pre = gates[..., :MLSTM_HEADS]
    log_f = jax.nn.log_sigmoid(gates[..., MLSTM_HEADS:])
    ht = _mlstm_cell_chunkwise(q, k, v, i_pre, log_f)
    ht = ht * lax.rsqrt(jnp.mean(jnp.square(ht), axis=-1, keepdims=True) + RMS_EPS)
    ht = ht.reshape(B, S, MLSTM_V_COLS) * head_gain.astype(jnp.float32)
    y = jax.nn.sigmoid(o.astype(jnp.float32)) * ht
    return y.astype(h.dtype) @ w_out

def _dilated_window_attention(q, k, v, window, dilation):
    B, S, H, Dh = q.shape
    blk = window // dilation
    unit = blk * dilation
    s_pad = -(-S // unit) * unit
    nb = s_pad // unit

    def to_blocks(t):
        t = jnp.pad(t.astype(jnp.float32), ((0, 0), (0, s_pad - S), (0, 0), (0, 0)))
        t = jnp.swapaxes(t.reshape(B, s_pad // dilation, dilation, H, Dh), 1, 2)
        return t.reshape(B, dilation, nb, blk, H, Dh)

    def with_prev(t):
        prev = jnp.pad(t, ((0, 0), (0, 0), (1, 0), (0, 0), (0, 0), (0, 0)))[:, :, :-1]
        return jnp.concatenate([prev, t], axis=3)

    qb = to_blocks(q)
    kc = with_prev(to_blocks(k))
    vc = with_prev(to_blocks(v))
    s = jnp.einsum('brnqhd,brnkhd->brnhqk', qb, kc) * (Dh ** -0.5)
    qi = jnp.arange(blk)[:, None]
    ki = jnp.arange(2 * blk)[None, :]
    band = (ki >= qi) & (ki <= qi + blk)
    has_prev = (jnp.arange(nb) > 0)[:, None, None] | (ki >= blk)[None]
    mask = band[None] & has_prev
    s = jnp.where(mask[:, None], s, -jnp.inf)
    mx = s.max(-1, keepdims=True)
    e = jnp.exp(s - mx)
    den = e.sum(-1)
    o = jnp.einsum('brnhqk,brnkhd->brnqhd', e, vc) / jnp.swapaxes(den, 3, 4)[..., None]
    lse = jnp.swapaxes(mx[..., 0] + jnp.log(den), 3, 4)

    def from_blocks(t):
        t = t.reshape((B, dilation, s_pad // dilation) + t.shape[4:])
        t = jnp.swapaxes(t, 1, 2).reshape((B, s_pad) + t.shape[3:])
        return t[:, :S]

    return from_blocks(o), from_blocks(lse)

def _dilated_mixer(h, w_in, w_out):
    B, S, _ = h.shape
    proj = (h @ w_in).reshape(B, S, N_GROUPS, 3, ATTN_HEADS, ATTN_HEAD_DIM)
    outs, lses = [], []
    for g, (window, dilation) in enumerate(DIL_GROUPS):
        o_g, lse_g = _dilated_window_attention(proj[:, :, g, 0], proj[:, :, g, 1], proj[:, :, g, 2], window, dilation)
        outs.append(o_g)
        lses.append(lse_g)
    wts = jax.nn.softmax(jnp.stack(lses, 0), axis=0)
    o = jnp.sum(wts[..., None] * jnp.stack(outs, 0), axis=0)
    return o.reshape(B, S, ATTN_HEADS * ATTN_HEAD_DIM).astype(h.dtype) @ w_out

def _dense(key, fan_in, shape, scale=1.0):
    return jax.random.normal(key, shape, jnp.float32) * (scale * fan_in ** -0.5)

def setup_inputs(seed: int = 0) -> dict:
    key = jax.random.key(seed)
    ks = jax.random.split(key, 20)
    na, nb_ = N_MLSTM_LAYERS, N_ATTN_LAYERS
    x = jax.random.normal(ks[0], (BATCH, SEQ, D_MODEL), jnp.float32)
    c = jax.random.normal(ks[1], (BATCH, D_MODEL), jnp.float32)
    ada_w = _dense(ks[2], D_MODEL, (DEPTH, D_MODEL, N_SUB * 3 * D_MODEL), 0.1)
    ada_b = 0.01 * jax.random.normal(ks[3], (DEPTH, N_SUB * 3 * D_MODEL), jnp.float32)
    ln_g = 1.0 + 0.02 * jax.random.normal(ks[4], (DEPTH, N_SUB, D_MODEL), jnp.float32)
    ln_b = 0.02 * jax.random.normal(ks[5], (DEPTH, N_SUB, D_MODEL), jnp.float32)
    ffn_w_in = _dense(ks[6], D_MODEL, (DEPTH, 2, D_MODEL, 2 * D_FF))
    ffn_w_out = _dense(ks[7], D_FF, (DEPTH, 2, D_FF, D_MODEL), BETA)
    mlstm_w_in = jnp.concatenate([
        _dense(ks[8], D_MODEL, (na, D_MODEL, MLSTM_QK_COLS)),
        _dense(ks[9], D_MODEL, (na, D_MODEL, MLSTM_V_COLS), BETA),
        _dense(ks[10], D_MODEL, (na, D_MODEL, MLSTM_V_COLS + 2 * MLSTM_HEADS)),
    ], axis=-1)
    mlstm_gate_bias = jnp.concatenate([
        0.1 * jax.random.normal(ks[11], (na, MLSTM_HEADS), jnp.float32),
        3.0 + 3.0 * jax.random.uniform(ks[12], (na, MLSTM_HEADS), jnp.float32),
    ], axis=-1)
    mlstm_conv_w = _dense(ks[13], CONV_WIDTH, (na, CONV_WIDTH, MLSTM_QK_COLS))
    mlstm_head_gain = 1.0 + 0.02 * jax.random.normal(ks[14], (na, MLSTM_V_COLS), jnp.float32)
    mlstm_w_out = _dense(ks[15], MLSTM_V_COLS, (na, MLSTM_V_COLS, D_MODEL), BETA)
    qkv_scale = jnp.array([1.0, 1.0, BETA], jnp.float32)[:, None]
    attn_w_in = (_dense(ks[16], D_MODEL, (nb_, D_MODEL, N_GROUPS, 3, ATTN_HEADS * ATTN_HEAD_DIM)) * qkv_scale
                 ).reshape(nb_, D_MODEL, ATTN_PROJ)
    attn_w_out = _dense(ks[17], ATTN_HEADS * ATTN_HEAD_DIM, (nb_, ATTN_HEADS * ATTN_HEAD_DIM, D_MODEL), BETA)
    return {'x': x, 'c': c, 'ada_w': ada_w, 'ada_b': ada_b, 'ln_g': ln_g, 'ln_b': ln_b,
            'ffn_w_in': ffn_w_in, 'ffn_w_out': ffn_w_out, 'mlstm_w_in': mlstm_w_in,
            'mlstm_gate_bias': mlstm_gate_bias, 'mlstm_conv_w': mlstm_conv_w,
            'mlstm_head_gain': mlstm_head_gain, 'mlstm_w_out': mlstm_w_out,
            'attn_w_in': attn_w_in, 'attn_w_out': attn_w_out}

def reference(x, c, ada_w, ada_b, ln_g, ln_b, ffn_w_in, ffn_w_out, mlstm_w_in, mlstm_gate_bias,
              mlstm_conv_w, mlstm_head_gain, mlstm_w_out, attn_w_in, attn_w_out):
    B = x.shape[0]
    cond = jax.nn.silu(c)
    for layer in range(DEPTH):
        mod = (cond @ ada_w[layer] + ada_b[layer]).reshape(B, N_SUB, 3, 1, D_MODEL)

        def modulate(h, s):
            return h * (1.0 + mod[:, s, 1]) + mod[:, s, 0]

        def post(h, out, s, weight):
            return _layer_norm(ALPHA * h + weight * (1.0 + mod[:, s, 2]) * out, ln_g[layer, s], ln_b[layer, s])

        x = post(x, _swiglu(modulate(x, 0), ffn_w_in[layer, 0], ffn_w_out[layer, 0]), 0, 0.5)
        j = layer // N_MIXERS
        if layer % N_MIXERS == 0:
            y = _mlstm_mixer(modulate(x, 1), mlstm_w_in[j], mlstm_gate_bias[j], mlstm_conv_w[j],
                             mlstm_head_gain[j], mlstm_w_out[j])
        else:
            y = _dilated_mixer(modulate(x, 1), attn_w_in[j], attn_w_out[j])
        x = post(x, y, 1, 1.0)
        x = post(x, _swiglu(modulate(x, 2), ffn_w_in[layer, 1], ffn_w_out[layer, 1]), 2, 0.5)
    return x


_drawn_inputs = setup_inputs


def setup_inputs(seed=0):
    import zlib

    import numpy as np

    out = dict(_drawn_inputs(seed))
    spreads = {}
    factors = {'ada_b': 5.34, 'mlstm_head_gain': 8.0}
    for name, (base, spread) in spreads.items():
        noise = np.random.default_rng([zlib.crc32(name.encode()), seed]).standard_normal(out[name].shape)
        drawn = base * np.exp(spread * noise) if base else spread * noise
        out[name] = __import__('jax').numpy.asarray(drawn.astype(out[name].dtype))
    for name, factor in factors.items():
        out[name] = (out[name] * factor).astype(out[name].dtype)
    return out
```

```python
import math
from contextlib import ExitStack

import concourse.bass as bass
from concourse import mybir

F32 = mybir.dt.float32
F32R = mybir.dt.float32r
ALU = mybir.AluOpType
ACT = mybir.ActivationFunctionType
AX = mybir.AxisListType

P = 128
D_MODEL = 1024
SEQ = 512
D_FF = 2816
DEPTH = 2
N_SUB = 3
NLAYERS = DEPTH * N_SUB
HEADS = 8
DQK = 64
KD = D_MODEL // P
NF = D_FF // P
NB = SEQ // P
ALPHA = (2 * DEPTH) ** 0.25
LN_EPS = 1e-5
RMS_EPS = 1e-6
V_COL = 2 * HEADS * DQK
O_COL = V_COL + D_MODEL
GATE_COL = O_COL + D_MODEL
GROUP_COLS = 3 * D_MODEL
DIL = 4
SCALE = P ** -0.5
MASKED = -1e30

RING = 4
ATT_RING = 3
K_CHUNKS = [(0, 8), (8, 8), (16, 6)]
FFN_UNITS = 2 * NF + len(K_CHUNKS) * KD
MLSTM_UNITS = 4 * KD
HEAD_UNITS = [(0, 0), (0, 1), (1, 0), (1, 1), (2, 0), (2, 1), (0, 2), (1, 2), (2, 2)]
ATT_HEAD_UNITS = len(HEAD_UNITS) * HEADS
FIRST = [0]
for _size in (FFN_UNITS, MLSTM_UNITS, FFN_UNITS, FFN_UNITS, ATT_HEAD_UNITS + KD, FFN_UNITS):
    FIRST.append(FIRST[-1] + _size)
N_UNITS = FIRST[-1]
ATT0, ATT1 = FIRST[4], FIRST[4] + ATT_HEAD_UNITS

CHUNK = 512
CHUNKS = N_SUB * 3 * D_MODEL // CHUNK
ADA_RING = 4
UPFRONT = 4

HALF = SEQ // 2
JOIN = (0, 0, 1, 3)

ATT_BLOCKS = 15
G1_COL, G2_COL = 7 * P, 11 * P

SEG = [0, 512, 896, 1152, 1280]


class Pos:

    def __init__(self, first, step=0, i=None):
        self.first, self.step, self.i = first, step, i

    def __add__(self, n):
        return Pos(self.first + n, self.step, self.i)

    def __sub__(self, n):
        return self + -n

    def __mul__(self, n):
        return Pos(self.first * n, self.step * n, self.i)

    def __floordiv__(self, n):
        assert self.step % n == 0
        return Pos(self.first // n, self.step // n, self.i)

    def __mod__(self, n):
        assert self.step % n == 0
        return self.first % n

    @property
    def at(self):
        return self.i * self.step + self.first if self.step else self.first


def at(first, step, i):
    return Pos(first, step, i) if i is not None else Pos(first)


def pos(x):
    return x if isinstance(x, Pos) else Pos(x)


def wait(eng, sem, count):
    count = pos(count)
    if count.step:
        assert count.first > 0, "a wait in a loop must be for a positive count"
    elif count.first <= 0:
        return
    eng.wait_ge(sem, count.at)


def one(index):
    return bass.ds(pos(index).at, 1)


def slot_of(u):
    u = pos(u)
    return (u - ATT0) % ATT_RING if ATT0 <= u.first < ATT1 else u % RING


def fill_of(u):
    u = pos(u)
    if u.first < ATT0:
        return u // RING + 1
    if u.first < ATT1:
        return (u - ATT0) // ATT_RING + (ATT0 // RING + 1)
    extra = ATT_HEAD_UNITS // ATT_RING if (u - ATT1) % RING < ATT_RING else 0
    return (u - ATT1) // RING + (ATT0 // RING + extra + 1)


def units_before(u):
    u = pos(u)
    if ATT0 + ATT_RING <= u.first < ATT1 + ATT_RING:
        return u - (ATT_RING - 1)
    if u.first == ATT1 + ATT_RING:
        return pos(0)
    return u - (RING - 1)


def trunk(nc, x, c, ada_w, ada_b, ln_g, ln_b, ffn_w_in, ffn_w_out, mlstm_w_in, mlstm_gate_bias,
          mlstm_conv_w, mlstm_head_gain, mlstm_w_out, attn_w_in, attn_w_out, out):
    stack = ExitStack()
    with stack:
        def keep(ctx, name, shape, dt=F32):
            return ctx.enter_context(nc.sbuf_tensor(name, shape, dt))

        def sb(name, shape, dt=F32):
            return keep(stack, name, shape, dt)

        def sem(name):
            return stack.enter_context(nc.semaphore(name))

        xres = sb("xres", [P, KD, SEQ])
        xh = sb("xh", [P, KD, SEQ], F32R)
        xl = sb("xl", [P, KD, SEQ], F32R)
        w_raw = sb("w_raw", [P, RING, KD, P])
        w_hi = sb("w_hi", [P, RING, KD, P], F32R)
        w_lo = sb("w_lo", [P, RING, KD, P], F32R)
        ada_t = sb("ada_t", [P, ADA_RING, CHUNK])
        ada_acc = sb("ada_acc", [P, CHUNK])
        ident = sb("ident", [P, P])
        ones = sb("ones", [P, P])
        cols = sb("cols", [P, 3, P])
        mod = sb("mod", [P, NLAYERS * 3 * KD])
        gate_c = sb("gate_c", [P, NLAYERS * KD])
        mul_c = sb("mul_c", [P, NLAYERS * KD])
        add_c = sb("add_c", [P, NLAYERS * KD])
        cond = sb("cond", [P, KD])
        gbias = sb("gbias", [HEADS, 2])
        eps_c = sb("eps_c", [P, 1])
        ccol = sb("ccol", [P, NB, HEADS])
        mask = sb("mask", [P, 3, P])
        sel4 = sb("sel4", [P, DIL])
        token = sb("token", [1, 8])
        sq = sb("sq", [P, SEQ])
        st = sb("st", [P, 2, 5, 2])
        with ExitStack() as r:
            duo = keep(r, "duo", [P, 2, SEQ])
        acc = sb("acc", [P, 2, SEQ])
        with ExitStack() as r:
            xtok = keep(r, "xtok", [P, NB, D_MODEL])
            rows_t = keep(r, "rows_t", [P, 3, P])
            ada_first = keep(r, "ada_first", [P, KD, UPFRONT * CHUNK])
        with ExitStack() as r:
            hh = keep(r, "hh", [P, NF, SEQ], F32R)
            hl = keep(r, "hl", [P, NF, SEQ], F32R)
        with ExitStack() as r:
            sig = keep(r, "sig", [P, HEADS, SEQ])
            qk = keep(r, "qk", [P, KD, SEQ])
            vtok = keep(r, "vtok", [P, NB, D_MODEL])
            with ExitStack() as rr:
                g_raw = keep(rr, "g_raw", [P, KD, P])
                g_hi = keep(rr, "g_hi", [P, KD, P], F32R)
                g_lo = keep(rr, "g_lo", [P, KD, P], F32R)
                grow = keep(rr, "grow", [HEADS, 7, SEQ])
                decay = keep(rr, "decay", [HEADS, SEG[NB] + SEQ])
                conv = keep(rr, "conv", [P, 2, SEQ])
            with ExitStack() as rr:
                drow = keep(rr, "drow", [P, 2, SEG[NB] + SEQ])
                dmat = keep(rr, "dmat", [P, 2, SEG[NB]])
                nsq = keep(rr, "nsq", [P, SEQ])
                den = keep(rr, "den", [P, 2, SEQ])
                yv = keep(rr, "yv", [P, 2, SEQ])
        with ExitStack() as r:
            qT = keep(r, "qT", [P, 3, SEQ])
            kT = keep(r, "kT", [P, 3, SEQ])
            prob = keep(r, "prob", [P, ATT_BLOCKS, P])
            probT = keep(r, "probT", [P, ATT_BLOCKS, P])
            vt = keep(r, "vt", [P, 3, NB, P])
            yh = keep(r, "yh", [P, HEADS, SEQ], F32R)
            yl = keep(r, "yl", [P, HEADS, SEQ], F32R)
            yn = keep(r, "yn", [P, SEQ])
            mx = keep(r, "mx", [P, 3, NB])
            nb = keep(r, "nb", [P, 3, NB])
            dn = keep(r, "dn", [P, 3, NB])
            pm = keep(r, "pm", [P, 2, NB])
            pe12 = keep(r, "pe12", [P, 2, NB])
            pd = keep(r, "pd", [P, 2, NB])
            nm = keep(r, "nm", [P, 2, NB])
            ne = keep(r, "ne", [P, 2, NB])
            nd = keep(r, "nd", [P, 2, NB])
            nj = keep(r, "nj", [P, 2, NB])
            f12 = keep(r, "f12", [P, NB])
            pf = keep(r, "pf", [P, NB])
            fac = keep(r, "fac", [P, 3, NB])
        ln_t = acc[:, :, 0:HALF]
        ln_m = ada_acc[:, :].rearrange("p (j q) -> p j q", q=HALF)
        psum = stack.enter_context(nc.psum_tensor("psum", [P, 8, SEQ], F32))

        def y_of(h):
            return yv[:, h, :] if h < 2 else qk[:, h // 2 - 1 + (HEADS // 2) * (h % 2), :]

        decay_d = nc.dram_tensor("decay_d", [HEADS, SEG[NB] + SEQ], F32, kind="Internal").ap()
        joint_d = nc.dram_tensor("joint_d", [2, SEQ], F32, kind="Internal").ap()
        share_d = nc.dram_tensor("share_d", [SEQ], F32, kind="Internal").ap()

        s_rows = [sem("first_rows_in"), sem("more_rows_in")]
        s_xtok, s_gb = sem("xtok_in"), sem("gate_bias_in")
        s_const, s_mask, s_tok = sem("consts_made"), sem("mask_steps"), sem("start_values")
        s_colsT, s_cols, s_cond = sem("cols_transposed"), sem("cols_made"), sem("cond_made")
        s_xT = sem("x_transposed")
        s_raw = [sem(f"unit_in_slot{i}") for i in range(RING)]
        s_hi, s_lo, s_unit = sem("unit_high_made"), sem("unit_low_made"), sem("units_multiplied")
        s_first = [sem(f"ada_first_in{k}") for k in range(KD)]
        s_ada_in = [sem(f"ada_in_slot{i}") for i in range(ADA_RING)]
        s_ada, s_modp, s_mod, s_der = sem("ada_macs"), sem("mod_summed"), sem("mod_made"), sem("derived")
        s_xnew, s_xhi, s_xm, s_x = sem("xres_tiles"), sem("x_high"), sem("x_modulated"), sem("x_ready")
        s_sg, s_gu, s_hh, s_hl = sem("silu_gate"), sem("hidden"), sem("hidden_high"), sem("hidden_ready")
        s_z, s_sq, s_acc1, s_acc2 = sem("z_tiles"), sem("z_squares"), sem("z_sums"), sem("zz_sums")
        s_tail = sem("first_half_tiles")
        s_stat, s_mom, s_sd, s_rstd, s_bc = (sem("ln_sums"), sem("ln_moment_steps"), sem("ln_sd"),
                                             sem("ln_rstd"), sem("ln_rows_spread"))
        s_t, s_tn = sem("ln_centred"), sem("ln_normalised")
        s_ev = sem("projections_out")
        s_gin, s_gz, s_ghi, s_glo, s_gp = (sem("gate_w_in"), sem("gate_w_cleared"), sem("gate_w_high"),
                                           sem("gate_w_low"), sem("gates_multiplied"))
        s_gr, s_ga, s_row_st = sem("gate_row_steps"), sem("gate_row_act_steps"), sem("decay_stored")
        s_og, s_cx, s_qk = sem("output_gate_ready"), sem("conv_steps"), sem("qk_ready")
        s_cf = sem("conv_done")
        s_vt, s_vc = sem("v_transposed"), sem("v_ready")
        s_cT, s_cc = sem("ccol_transposed"), sem("ccol_ready")
        s_rb, s_rbc, s_dm = sem("decay_row_in"), sem("decay_masked"), sem("decay_matrix")
        s_S, s_SD, s_nd = sem("mlstm_scores"), sem("weighted_scores"), sem("num_den")
        s_ab = sem("den_abs")
        s_nsq, s_ms, s_dd, s_dsq, s_tt, s_sdm, s_rr, s_y1, s_y2, s_yh = (
            sem("num_squared"), sem("num_square_mean"), sem("den_bounded"), sem("den_squared"),
            sem("rms_sum"), sem("rms_root"), sem("rms_inverse"), sem("y_normed"), sem("y_gated"),
            sem("y_high"))
        s_yr = sem("y_ready")
        s_as, s_am, s_mxr, s_nb, s_ae = (sem("att_scores"), sem("att_masked"), sem("att_max"),
                                         sem("att_negmax"), sem("att_exp"))
        s_pc, s_pe, s_pst, s_pld, s_nc, s_ne, s_nst, s_nld, s_fac, s_sc = (
            sem("class_stats"), sem("class_exps"), sem("joint_stored"), sem("joint_in"),
            sem("token_stats"), sem("token_exps"), sem("share_stored"), sem("share_in"),
            sem("factor_steps"), sem("prob_scaled"))
        s_pt, s_pta, s_ptd = sem("prob_transposed"), sem("probT_by_act"), sem("probT_by_dve")
        s_o, s_on, s_oe = sem("att_out"), sem("att_out_copied"), sem("att_out_joined")
        s_fT, s_fo, s_fo2, s_out = (sem("out_transposed"), sem("out_by_act"), sem("out_by_dve"),
                                    sem("out_stored"))

        ffn_index = {0: 0, 2: 1, 3: 2, 5: 3}
        START = 2
        EV_START = 4

        def ev_before(n):
            return EV_START + (0 if n == 1 else 3 * KD)

        def ada_chunks(n):
            return {0: UPFRONT, 1: CHUNKS, 2: CHUNKS, 3: CHUNKS + NF // 2}.get(n, 2 * CHUNKS)

        def ada_rounds(n):
            return {0: NF // 2, 2: NF // 2, 3: CHUNKS - NF // 2}.get(n, 0)

        def der_before(n):
            return 2 + 4 * n

        def tail(n):
            return 1 if n in ffn_index else 2

        def d0(n):
            return KD - tail(n)

        def z_before(n):
            return START + sum(d0(k) + 2 * tail(k) for k in range(n))

        def sq_before(n):
            return z_before(n) - START

        def acc_before(n):
            return sum(1 + d0(k) + 2 * (tail(k) - 1) for k in range(n))

        def xnew_before(n):
            return KD + 2 * KD * n

        def tail_before(n):
            return sum(tail(k) for k in range(n))

        def tail_bank(n, half, i):
            return 5 - half if n in ffn_index else 4 + i

        def cols_of(half):
            return slice(half * HALF, (half + 1) * HALF)

        def tail_units(n):
            return 3 if n in ffn_index else 2

        def lead_limit(n):
            return ATT0 + ATT_RING if n == 3 else min(FIRST[n + 1] + RING, N_UNITS)

        w_in_v = [[ffn_w_in[l, j].rearrange("(k p) c -> p k c", p=P) for j in range(2)] for l in range(2)]
        w_out_v = [[ffn_w_out[l, j].rearrange("(k p) c -> p k c", p=P) for j in range(2)] for l in range(2)]
        ml_in_v = mlstm_w_in[0].rearrange("(k p) c -> p k c", p=P)
        ml_out_v = mlstm_w_out[0].rearrange("(k p) c -> p k c", p=P)
        at_in_v = attn_w_in[0].rearrange("(k p) c -> p k c", p=P)
        at_out_v = attn_w_out[0].rearrange("(k p) c -> p k c", p=P)

        def unit_source(u):
            u = pos(u)
            n = max(k for k in range(NLAYERS) if FIRST[k] <= u.first)
            m = u - FIRST[n]
            if n in ffn_index:
                l, j = n // N_SUB, (n % N_SUB) // 2
                if m.first < 2 * NF:
                    col = (m // 2) * P + (m % 2) * D_FF
                    return w_in_v[l][j][:, :, bass.ds(col.at, P)]
                m = m - 2 * NF
                k0, kt = K_CHUNKS[m % 3]
                return w_out_v[l][j][:, k0:k0 + kt, bass.ds(((m // 3) * P).at, P)]
            if n == 1:
                part = m.first // KD
                col = (m - part * KD) * P + (0, V_COL, O_COL, 0)[part]
                return (ml_in_v, ml_in_v, ml_in_v, ml_out_v)[part][:, :, bass.ds(col.at, P)]
            if m.first >= ATT_HEAD_UNITS:
                return at_out_v[:, :, bass.ds(((m - ATT_HEAD_UNITS) * P).at, P)]
            g, which = HEAD_UNITS[m % 9]
            col = (m // 9) * P + g * GROUP_COLS + which * D_MODEL
            return at_in_v[:, :, bass.ds(col.at, P)]

        def ada_share(c0, d):
            if d == 0:
                return c0 + NF // 2, range(KD)
            return c0 + NF // 2 + 1 + (d - 1) // 3, (range(0, 3), range(3, 6), range(6, 8))[(d - 1) % 3]

        block = stack.enter_context(nc.Block())

        @block.sync
        def _(sp):
            def load_unit(u):
                wait(sp, s_lo, units_before(u))
                src = unit_source(u)
                sp.dma_start(w_raw[:, slot_of(u), 0:src.shape[1], :], src).then_inc(s_raw[slot_of(u)], 16)

            def load_ada(ch, ks=range(KD)):
                ch = pos(ch)
                l = ch.first // CHUNKS
                for k in ks:
                    if ch.step or ch.first > UPFRONT or k >= ADA_RING:
                        wait(sp, s_ada, ch * KD + (k - ADA_RING + 1))
                    src = ada_w[l, k * P:(k + 1) * P, bass.ds(((ch - l * CHUNKS) * CHUNK).at, CHUNK)]
                    sp.dma_start(ada_t[:, k % ADA_RING, :], src).then_inc(s_ada_in[k % ADA_RING], 16)

            def load_first(k):
                sp.dma_start(ada_first[:, k, :], ada_w[0, k * P:(k + 1) * P, 0:UPFRONT * CHUNK]).then_inc(s_first[k], 16)

            def rows(dst, src):
                sp.dma_start(dst, src).then_inc(s_rows[0], 16)

            rows(rows_t[0:48, 0, :], ln_g.rearrange("l s (t q) -> (l s t) q", q=P))
            rows(rows_t[48:96, 0, :], ln_b.rearrange("l s (t q) -> (l s t) q", q=P))
            rows(rows_t[96:104, 0, :], c.rearrange("b (t q) -> (b t) q", q=P))
            rows(rows_t[104:112, 0, :], mlstm_head_gain.rearrange("b (t q) -> (b t) q", q=P))
            for k in range(4):
                load_first(k)
            sp.dma_start(xtok[:, :, :], x[0].rearrange("(b p) d -> p b d", p=P)).then_inc(s_xtok, 16)
            for k in (4, 5):
                load_first(k)
            for u in range(RING):
                load_unit(u)
            for k in (6, 7):
                load_first(k)

            def ffn(n):
                u0, c0 = FIRST[n], ada_chunks(n)

                def in_round(i, start, step):
                    for j in range(4):
                        load_unit(Pos(u0 + 4 + j + start, step, i))
                    if with_ada:
                        load_ada(Pos(c0 + start // 4, step // 4, i))

                with_ada = ada_rounds(n) > 0
                r = min(ada_rounds(n) or NF, NF // 2 - 1)
                with sp.Fori(0, r) as i:
                    in_round(i, 0, 4)
                with_ada = ada_rounds(n) == NF // 2
                if r < NF // 2 - 1:
                    with sp.Fori(0, NF // 2 - 1 - r) as i:
                        in_round(i, 4 * r, 4)
                in_round(None, 4 * (NF // 2 - 1), 0)
                o0 = u0 + 2 * NF
                for d in range(KD):
                    for q in range(3):
                        if o0 + 3 * d + 4 + q < lead_limit(n):
                            load_unit(o0 + 3 * d + 4 + q)
                    if n == 0 and d < d0(n):
                        load_ada(*ada_share(c0, d))

            def mlstm():
                u0 = FIRST[1]
                for m in range(MLSTM_UNITS):
                    load_unit(u0 + 4 + m)

            def attention():
                def head(t):
                    for j in range(9):
                        load_unit(t * 9 + (ATT0 + ATT_RING + j))
                with sp.Fori(0, HEADS - 1) as i:
                    head(Pos(0, 1, i))
                head(Pos(HEADS - 1))
                for d in range(-1, KD):
                    load_unit(ATT1 + d + 4)

            ffn(0)
            mlstm()
            ffn(2)
            ffn(3)
            attention()
            ffn(5)
            for b in range(NB):
                sp.wait_ge(s_fo, b + 1)
                sp.wait_ge(s_fo2, b + 1)
                sp.dma_start(out[0, b * P:(b + 1) * P, :], xtok[:, b, :]).then_inc(s_out, 16)
            sp.wait_ge(s_out, 16 * NB)

        @block.gpsimd
        def _(pool):
            for w in range(2):
                nc.gpsimd.dma_start(gbias[:, w:w + 1], mlstm_gate_bias[0, w * HEADS:(w + 1) * HEADS].unsqueeze(1)
                                    ).then_inc(s_gb, 16)
            nc.gpsimd.memset(ident[:, :], 0.0).then_inc(s_const, 1)
            nc.gpsimd.memset(ones[:, :], 1.0).then_inc(s_const, 1)
            nc.gpsimd.memset(eps_c[:, :], LN_EPS / ALPHA ** 2).then_inc(s_const, 1)
            nc.gpsimd.memset(mask[:, :, :], 0.0).then_inc(s_const, 1)
            pool.wait_ge(s_const, 4)
            nc.gpsimd.affine_select(out=ident[:, :], in_=ident[:, :], compare_op=ALU.not_equal, fill=1.0,
                                    base=0, pattern=[[-1, P]], channel_multiplier=1).then_inc(s_const, 1)
            nc.gpsimd.affine_select(out=mask[:, 0, :], in_=mask[:, 0, :], compare_op=ALU.is_ge, fill=MASKED,
                                    base=0, pattern=[[1, P]], channel_multiplier=-1).then_inc(s_const, 1)
            nc.gpsimd.affine_select(out=mask[:, 1, :], in_=mask[:, 1, :], compare_op=ALU.is_ge, fill=MASKED,
                                    base=0, pattern=[[-1, P]], channel_multiplier=1).then_inc(s_const, 1)

            def z_sums(n):
                tiles = [(d, slice(0, SEQ), d) for d in range(d0(n))]
                for half in range(2):
                    tiles += [(d0(n) + i, cols_of(half), d0(n) + tail(n) * half + i) for i in range(tail(n) - 1)]
                for a, (d, c, k) in enumerate(tiles):
                    pool.wait_ge(s_z, z_before(n) + k + 1)
                    pool.wait_ge(s_acc1, acc_before(n) + a + 1)
                    nc.gpsimd.tensor_tensor(acc[:, 0, c], acc[:, 0, c], xres[:, d, c], ALU.add).then_inc(s_acc1, 1)
                    pool.wait_ge(s_sq, sq_before(n) + k + 1)
                    pool.wait_ge(s_acc2, acc_before(n) + a + 1)
                    nc.gpsimd.tensor_tensor(acc[:, 1, c], acc[:, 1, c], sq[:, c], ALU.add).then_inc(s_acc2, 1)

            z_sums(0)
            pool.wait_ge(s_unit, FIRST[1])
            nc.gpsimd.memset(g_raw[:, :, :], 0.0).then_inc(s_gz, 1)
            pool.wait_ge(s_gz, 1)
            for w in range(2):
                nc.gpsimd.dma_start(g_raw[:, :, 32 * w:32 * w + HEADS],
                                    ml_in_v[:, :, GATE_COL + w * HEADS:GATE_COL + (w + 1) * HEADS]
                                    ).then_inc(s_gin, 16)
            pool.wait_ge(s_gr, GATE_ROW_STEPS)
            pool.wait_ge(s_ga, 4)
            nc.gpsimd.dma_start(decay_d, decay[:, :]).then_inc(s_row_st, 16)
            pool.wait_ge(s_row_st, 16)
            pool.wait_ge(s_cT, 1)
            pool.wait_ge(s_qk, START + KD)
            pool.wait_ge(s_gp, 1)
            for h in range(HEADS):
                if h >= 2:
                    pool.wait_ge(s_dd, h - 1)
                    pool.wait_ge(s_dm, 4 * (h - 1))
                nc.gpsimd.dma_start(drow[:, h % 2, :], decay_d[h].partition_broadcast(P)).then_inc(s_rb, 16)
                pool.wait_ge(s_rb, 16 * (h + 1))
                for j in range(NB):
                    seg = drow[:, h % 2, SEG[j]:SEG[j] + P]
                    nc.gpsimd.affine_select(out=seg, in_=seg, compare_op=ALU.is_ge, fill=MASKED, base=0,
                                            pattern=[[1, P]], channel_multiplier=-1).then_inc(s_rbc, 1)

            z_sums(1)
            z_sums(2)
            z_sums(3)

            def exchange(t):
                wait(pool, s_pc, t * 6 + 6)
                nc.gpsimd.dma_start(joint_d.rearrange("a (i r) -> i a r", r=NB), pm[:, :, :]).then_inc(s_pst, 16)
                wait(pool, s_pst, t * 16 + 16)
                nc.gpsimd.dma_start(nm[:, :, :], joint_d.rearrange("a (b p) -> p a b", p=P),
                                    allow_slow_non_contiguous=True).then_inc(s_pld, 16)
                wait(pool, s_nc, t * 8 + 8)
                nc.gpsimd.dma_start(share_d.rearrange("(b p) -> p b", p=P), f12[:, :],
                                    allow_slow_non_contiguous=True).then_inc(s_nst, 16)
                wait(pool, s_nst, t * 16 + 16)
                nc.gpsimd.dma_start(pf[:, :], share_d.rearrange("(i r) -> i r", r=NB)).then_inc(s_nld, 16)

            for t in range(HEADS):
                exchange(Pos(t))
            z_sums(4)
            z_sums(5)

        @block.scalar
        def _(act):
            def high(u):
                s = slot_of(u)
                wait(act, s_raw[s], fill_of(u) * 16)
                wait(act, s_unit, units_before(u))
                nc.scalar.activation(w_hi[:, s], w_raw[:, s], ACT.Copy).then_inc(s_hi, 1)

            def square(n, d):
                wait(act, s_z, d + (z_before(n) + 1))
                wait(act, s_acc2, d + (acc_before(n) + 1))
                nc.scalar.activation(sq[:, :], xres[:, one(d), :], ACT.Square).then_inc(s_sq, 1)

            def tail_squares(n, half):
                for i in range(tail(n)):
                    act.wait_ge(s_z, z_before(n) + d0(n) + tail(n) * half + i + 1)
                    act.wait_ge(s_acc2, acc_before(n) + 1 + d0(n) + (tail(n) - 1) * half + i)
                    nc.scalar.activation(sq[:, cols_of(half)], xres[:, d0(n) + i, cols_of(half)], ACT.Square
                                         ).then_inc(s_sq, 1)

            def ln_root(n, half):
                act.wait_ge(s_mom, 3 * (2 * n + half + 1))
                nc.scalar.activation(st[:, half, 3, :], st[:, half, 2, :], ACT.Sqrt, bias=eps_c[:, :]
                                     ).then_inc(s_sd, 1)

            def high_x(n, half, d, src):
                nc.scalar.activation(xh[:, d, cols_of(half)], src, ACT.Identity,
                                     bias=add_c[:, d + n * KD:d + n * KD + 1],
                                     scale=mul_c[:, d + n * KD:d + n * KD + 1]).then_inc(s_xhi, 1)

            def ln_tiles(n, half, ds):
                for d in ds:
                    src = ln_t[:, d % 2, :]
                    act.wait_ge(s_tn, 2 * KD * n + KD * half + d + 1)
                    if n + 1 < NLAYERS:
                        high_x(n + 1, half, d, src)
                    nc.scalar.activation(xres[:, d, cols_of(half)], src, ACT.Identity,
                                         bias=cols[:, 0, 48 + n * KD + d:49 + n * KD + d],
                                         scale=cols[:, 0, n * KD + d:n * KD + d + 1]).then_inc(s_xnew, 1)

            def layer_norm(n):
                lead = [u for u in range(FIRST[n + 1] + 4 - tail_units(n), FIRST[n + 1] + 4) if u < lead_limit(n)]
                tail_squares(n, 0)
                if tail_units(n) == 3 and lead:
                    high(lead.pop(0))
                ln_root(n, 0)
                if lead:
                    high(lead.pop(0))
                ln_tiles(n, 0, (0, 1))
                tail_squares(n, 1)
                if lead:
                    high(lead.pop(0))
                ln_tiles(n, 0, (2, 3))
                ln_root(n, 1)
                ln_tiles(n, 0, range(4, KD))
                ln_tiles(n, 1, range(KD))

            def ffn(n):
                u0, h0 = FIRST[n], NF * ffn_index[n]
                act.wait_ge(s_xnew, xnew_before(n))

                with act.Fori(0, NF // 2) as i:
                    for j in range(2):
                        f = Pos(j, 2, i)
                        u = Pos(u0 + 2 * j, 4, i)
                        wait(act, s_unit, u + 1)
                        wait(act, s_hl, f + (START + h0 - 1))
                        nc.scalar.activation(duo[:, j, :], psum[:, 2 * j, :], ACT.Silu).then_inc(s_sg, 1)
                        high(u + 4)
                        wait(act, s_gu, f + (START + h0 + 1))
                        nc.scalar.activation(hh[:, one(f), :], duo[:, j:j + 1, :], ACT.Copy).then_inc(s_hh, 1)
                        high(u + 5)

                for d in range(d0(n)):
                    u = u0 + 2 * NF + 3 * d
                    high(u + 4)
                    high(u + 5)
                    square(n, d)
                    if u + 6 < lead_limit(n):
                        high(u + 6)
                layer_norm(n)

            def gates():
                act.wait_ge(s_gr, 3)
                nc.scalar.activation(grow[:, 2, :], grow[:, 1, :], ACT.Abs).then_inc(s_ga, 1)
                act.wait_ge(s_ga, 1)
                nc.scalar.activation(grow[:, 2, :], grow[:, 2, :], ACT.Exp, scale=-1.0).then_inc(s_ga, 1)
                act.wait_ge(s_ga, 2)
                nc.scalar.activation(grow[:, 2, :], grow[:, 2, :], ACT.Ln, bias=ones[0:HEADS, 0:1]).then_inc(s_ga, 1)
                act.wait_ge(s_gr, 7)
                nc.scalar.activation(decay[:, SEG[NB]:], grow[:, 5, :], ACT.Exp, scale=-1.0).then_inc(s_ga, 1)

            def mlstm():
                n, u0, e0 = 1, FIRST[1], ev_before(1)
                act.wait_ge(s_xnew, xnew_before(n))
                act.wait_ge(s_gin, 32)
                nc.scalar.activation(g_hi[:, :, :], g_raw[:, :, :], ACT.Copy).then_inc(s_ghi, 1)
                for half in range(2):
                    for j in range(4):
                        m = 4 * half + j
                        act.wait_ge(s_unit, u0 + m + 1)
                        act.wait_ge(s_cf, m + START - 1)
                        nc.scalar.activation(duo[:, j % 2, :], psum[:, j, :], ACT.Copy).then_inc(s_ev, 1)
                        high(u0 + m + 4)
                        act.wait_ge(s_cf, m + START + 1)
                        nc.scalar.activation(qk[:, m, :], conv[:, j % 2, :], ACT.Silu).then_inc(s_qk, 1)
                    if half == 0:
                        gates()
                with act.Fori(0, 2) as i:
                    for j in range(4):
                        m = Pos(KD + j, 4, i)
                        wait(act, s_unit, m + (u0 + 1))
                        wait(act, s_vt, m - KD + (START - 1))
                        nc.scalar.activation(duo[:, j % 2, :], psum[:, j, :], ACT.Copy).then_inc(s_ev, 1)
                        high(m + (u0 + 4))

                def gate_out(h):
                    act.wait_ge(s_unit, u0 + 2 * KD + h + 1)
                    nc.scalar.activation(sig[:, h, :], psum[:, 6, :], ACT.Copy).then_inc(s_ev, 1)
                    high(u0 + 2 * KD + h + 4)

                def decay_matrix(h):
                    if h >= 2:
                        act.wait_ge(s_nd, h - 1)
                    act.wait_ge(s_rbc, 4 * (h + 1))
                    for b in range(NB):
                        nc.scalar.activation(dmat[:, h % 2, SEG[b]:SEG[b + 1]], drow[:, h % 2, SEG[b]:SEG[b + 1]],
                                             ACT.Exp, bias=ccol[:, b, h:h + 1]).then_inc(s_dm, 1)

                gate_out(0)
                act.wait_ge(s_cc, 1)
                decay_matrix(0)
                gate_out(1)
                for h in range(HEADS):
                    if h + 1 < HEADS:
                        decay_matrix(h + 1)
                    act.wait_ge(s_nd, h + 1)
                    if h >= 1:
                        act.wait_ge(s_ms, h)
                    nc.scalar.activation(nsq[:, :], psum[:, 3 + h % 2, :], ACT.Square).then_inc(s_nsq, 1)
                    if h >= 2:
                        act.wait_ge(s_y1, h - 1)
                    nc.scalar.activation(den[:, h % 2, :], psum[:, 5, :], ACT.Abs).then_inc(s_ab, 1)
                    act.wait_ge(s_dd, h + 1)
                    nc.scalar.activation(den[:, h % 2, :], den[:, h % 2, :], ACT.Square,
                                         scale=math.sqrt(RMS_EPS)).then_inc(s_dsq, 1)
                    if h + 2 < HEADS - 1:
                        gate_out(h + 2)
                    act.wait_ge(s_tt, h + 1)
                    nc.scalar.activation(den[:, h % 2, :], den[:, h % 2, :], ACT.Sqrt).then_inc(s_sdm, 1)

                def sigmoid(h):
                    nc.scalar.activation(sig[:, h, :], sig[:, h, :], ACT.Sigmoid).then_inc(s_og, 1)

                act.wait_ge(s_ev, e0 + 3 * KD - 1)
                for h in range(3):
                    sigmoid(h)
                gate_out(HEADS - 1)
                act.wait_ge(s_ev, e0 + 3 * KD)
                for h in range(HEADS):
                    act.wait_ge(s_y2, h + 1)
                    nc.scalar.activation(xh[:, h, :], y_of(h), ACT.Copy).then_inc(s_yh, 1)
                    if h + 3 < HEADS:
                        sigmoid(h + 3)

                for d in range(d0(n)):
                    high(u0 + 3 * KD + 4 + d)
                    square(n, d)
                layer_norm(n)

            def attention():
                n, e0 = 4, ev_before(4)
                act.wait_ge(s_xnew, xnew_before(n))

                def head(t, prev):
                    for j in range(9):
                        m = t * 9 + j
                        g, which = HEAD_UNITS[j]
                        wait(act, s_unit, m + (ATT0 + 1))
                        src = psum[:, j % 3, :]
                        if g:
                            src = src.rearrange("p (i r) -> p r i", r=DIL)
                        if which < 2:
                            if which == 0 and g == 0:
                                wait(act, s_as, t)
                            dst = (qT, kT)[which][:, g, :]
                        else:
                            wait(act, s_vt, t * 3 + (START + KD + g - 1))
                            dst = duo[:, g % 2, :]
                        if g:
                            dst = dst.rearrange("p (r i) -> p r i", r=DIL)
                        nc.scalar.activation(dst, src, ACT.Copy).then_inc(s_ev, 1)
                        high(m + (ATT0 + ATT_RING))
                        if prev is not None:
                            if j == 0:
                                class_exps(prev)
                            if j == 2:
                                token_exps(prev)
                            if j == 4:
                                prob_out(prev)
                            if j == 5:
                                out_copy(prev)
                            if j == 6:
                                out_high(prev)
                        if j == 7:
                            exps(t)

                def exps(t):
                    wait(act, s_nb, t + 1)
                    for g in range(3):
                        for b in range(NB):
                            if g == 0:
                                lo, n_b = (0, 1) if b == 0 else (2 * b - 1, 2)
                            else:
                                lo, n_b = (7, 11)[g - 1] + b, 1
                            blk = prob[:, lo:lo + n_b, :]
                            nc.scalar.activation(blk, blk, ACT.Exp, bias=nb[:, g, b:b + 1], scale=SCALE,
                                                 accum_out=dn[:, g, b:b + 1]).then_inc(s_ae, 1)

                def class_exps(t):
                    wait(act, s_pc, t * 6 + 3)
                    nc.scalar.activation(pe12[:, :, :], pd[:, :, :], ACT.Exp, scale=SCALE).then_inc(s_pe, 1)

                def token_exps(t):
                    wait(act, s_nc, t * 8 + 3)
                    nc.scalar.activation(ne[:, :, :], nj[:, :, :], ACT.Exp, scale=SCALE).then_inc(s_ne, 1)

                def prob_out(t):
                    wait(act, s_pt, t + 1)
                    for bank in (3, 5):
                        b0 = (bank - 3) * 4
                        nc.scalar.activation(probT[:, b0:b0 + 4, :].rearrange("p b q -> p (b q)"),
                                             psum[:, bank, :], ACT.Copy).then_inc(s_pta, 1)

                def out_copy(t):
                    wait(act, s_o, t + 1)
                    nc.scalar.activation(yn[:, :], psum[:, 7, :], ACT.Copy).then_inc(s_on, 1)

                def out_high(t):
                    wait(act, s_oe, t + 1)
                    nc.scalar.activation(yh[:, one(t), :], yn[:, :].unsqueeze(1), ACT.Copy).then_inc(s_yh, 1)

                head(Pos(0), None)
                with act.Fori(0, HEADS - 1) as i:
                    head(Pos(1, 1, i), Pos(0, 1, i))
                t = Pos(HEADS - 1)
                class_exps(t)
                high(ATT1 + ATT_RING)
                token_exps(t)
                prob_out(t)
                out_copy(t)
                out_high(t)
                for d in range(d0(n)):
                    high(ATT1 + 4 + d)
                    square(n, d)
                layer_norm(n)

            def rows(dst, src):
                act.dma_start(dst, src).then_inc(s_rows[1], 16)

            rows(rows_t[0:72, 1, :], ada_b[0].rearrange("(t q) -> t q", q=P))
            rows(rows_t[72:104, 1, :], mlstm_conv_w[0].rearrange("j (t q) -> (j t) q", q=P))
            rows(rows_t[0:72, 2, :], ada_b[1].rearrange("(t q) -> t q", q=P))
            act.wait_ge(s_cols, 1)
            nc.scalar.activation(cond[:, :], cols[:, 0, 96:104], ACT.Silu).then_inc(s_cond, 1)
            for d in range(KD):
                act.wait_ge(s_xT, d + 1)
                nc.scalar.activation(xres[:, d, :], psum[:, d % 4, :], ACT.Copy).then_inc(s_xnew, 1)
            for u in range(RING):
                high(u)
            act.wait_ge(s_der, 2)
            for half in range(2):
                for d in range(KD):
                    act.wait_ge(s_xnew, d + 1)
                    high_x(0, half, d, xres[:, d, cols_of(half)])
            ffn(0)
            mlstm()
            ffn(2)
            ffn(3)
            attention()
            ffn(5)
            for b in range(NB):
                act.wait_ge(s_fT, 2 * b + 1)
                nc.scalar.activation(xtok[:, b, 0:SEQ], psum[:, 2 * b, :], ACT.Copy).then_inc(s_fo, 1)

        @block.vector
        def _(dve):
            def low(u):
                s = slot_of(u)
                wait(dve, s_hi, pos(u) + 1)
                nc.vector.tensor_tensor(w_lo[:, s], w_raw[:, s], w_hi[:, s].bitcast(F32),
                                        ALU.subtract).then_inc(s_lo, 1)

            def ada(ch, ks=range(KD)):
                ch = pos(ch)
                for k in ks:
                    s = k % ADA_RING
                    wait(dve, s_ada_in[s], (ch - UPFRONT) * 32 + 16 * (k // ADA_RING + 1))
                    if k == 0:
                        wait(dve, s_modp, ch)
                        nc.vector.tensor_scalar(ada_acc[:, :], ada_t[:, s, :], cond[:, 0:1], None,
                                                ALU.mult).then_inc(s_ada, 1)
                    else:
                        wait(dve, s_ada, ch * KD + k)
                        nc.vector.scalar_tensor_tensor(out=ada_acc[:, :], in0=ada_t[:, s, :],
                                                       scalar=cond[:, k:k + 1], in1=ada_acc[:, :],
                                                       op0=ALU.mult, op1=ALU.add).then_inc(s_ada, 1)

            def mod_column(ch):
                ch = pos(ch)
                l = ch.first // CHUNKS
                wait(dve, s_modp, ch + 1)
                nc.vector.tensor_tensor(mod[:, bass.ds((ch * 4).at, 4)], psum[:, 7, 0:4],
                                        cols[:, 1 + l, bass.ds(((ch - l * CHUNKS) * 4).at, 4)],
                                        ALU.add).then_inc(s_mod, 1)

            def derive(n, weight):
                c0, d0 = 3 * KD * n, der_before(n)
                wait(dve, s_mod, min((c0 + 5 * KD) // 4, 2 * CHUNKS))
                nc.vector.tensor_scalar(gate_c[:, n * KD:(n + 1) * KD], mod[:, c0 + 2 * KD:c0 + 3 * KD], 1.0,
                                        weight / ALPHA, ALU.add, ALU.mult).then_inc(s_der, 1)
                if n + 1 == NLAYERS:
                    return
                c1, k1 = c0 + 3 * KD, (n + 1) * KD
                nc.vector.scalar_tensor_tensor(out=mul_c[:, k1:k1 + KD], in0=mod[:, c1 + KD:c1 + 2 * KD],
                                               scalar=1.0, in1=cols[:, 0, n * KD:(n + 1) * KD],
                                               op0=ALU.add, op1=ALU.mult).then_inc(s_der, 1)
                nc.vector.scalar_tensor_tensor(out=add_c[:, k1:k1 + KD], in0=mod[:, c1 + KD:c1 + 2 * KD],
                                               scalar=1.0, in1=cols[:, 0, 48 + n * KD:48 + (n + 1) * KD],
                                               op0=ALU.add, op1=ALU.mult).then_inc(s_der, 1)
                dve.wait_ge(s_der, d0 + 3)
                nc.vector.tensor_tensor(add_c[:, k1:k1 + KD], add_c[:, k1:k1 + KD], mod[:, c1:c1 + KD],
                                        ALU.add).then_inc(s_der, 1)

            def clear_sums(n):
                dve.wait_ge(s_der, der_before(n) + 1)
                nc.vector.memset(acc[:, 0, :], 0.0).then_inc(s_acc1, 1)
                nc.vector.memset(acc[:, 1, :], 0.0).then_inc(s_acc2, 1)

            def z_tile(n, d, bank, unit):
                dve.wait_ge(s_unit, unit + 1)
                dve.wait_ge(s_xnew, xnew_before(n))
                nc.vector.scalar_tensor_tensor(out=xres[:, d, :], in0=psum[:, bank, :],
                                               scalar=gate_c[:, n * KD + d:n * KD + d + 1], in1=xres[:, d, :],
                                               op0=ALU.mult, op1=ALU.add).then_inc(s_z, 1)

            def z_tail(n, half, unit):
                c = cols_of(half)
                for i in range(tail(n)):
                    d = d0(n) + i
                    if half == 0:
                        dve.wait_ge(s_tail, tail_before(n) + i + 1)
                    else:
                        dve.wait_ge(s_unit, unit + i + 1)
                    nc.vector.scalar_tensor_tensor(out=xres[:, d, c], in0=psum[:, tail_bank(n, half, i), c],
                                                   scalar=gate_c[:, n * KD + d:n * KD + d + 1], in1=xres[:, d, c],
                                                   op0=ALU.mult, op1=ALU.add).then_inc(s_z, 1)

            def ln_moments(n, half):
                k = 3 * (2 * n + half)
                dve.wait_ge(s_stat, 2 * n + half + 1)
                nc.vector.tensor_scalar(st[:, half, 0, :], psum[:, 6 + half, 0:2], -1 / D_MODEL, None, ALU.mult
                                        ).then_inc(s_mom, 1)
                dve.wait_ge(s_mom, k + 1)
                nc.vector.tensor_tensor(st[:, half, 1, :], st[:, half, 0, :], st[:, half, 0, :], ALU.mult
                                        ).then_inc(s_mom, 1)
                dve.wait_ge(s_mom, k + 2)
                nc.vector.scalar_tensor_tensor(out=st[:, half, 2, :], in0=psum[:, 6 + half, 2:4], scalar=1 / D_MODEL,
                                               in1=st[:, half, 1, :], op0=ALU.mult, op1=ALU.subtract
                                               ).then_inc(s_mom, 1)

            def ln_inverse(n, half):
                dve.wait_ge(s_sd, 2 * n + half + 1)
                nc.vector.reciprocal(st[:, half, 4, :], st[:, half, 3, :]).then_inc(s_rstd, 1)

            def low_x(n, half, d, src):
                k = 2 * KD * n + KD * half + d + 1
                nc.vector.tensor_scalar(ln_m[:, d % 2, :], src, mul_c[:, d + n * KD:d + n * KD + 1],
                                        add_c[:, d + n * KD:d + n * KD + 1], ALU.mult, ALU.add).then_inc(s_xm, 1)
                dve.wait_ge(s_xm, k)
                dve.wait_ge(s_xhi, k)
                nc.vector.tensor_tensor(xl[:, d, cols_of(half)], ln_m[:, d % 2, :],
                                        xh[:, d, cols_of(half)].bitcast(F32), ALU.subtract).then_inc(s_x, 1)

            def ln_tiles(n, half, ds):
                k = 2 * KD * n + KD * half
                for a in ds[::2]:
                    for d in (a, a + 1):
                        if n + 1 < NLAYERS:
                            dve.wait_ge(s_xhi, 2 * KD + k + d - 1)
                        dve.wait_ge(s_xnew, KD + k + d - 1)
                        dve.wait_ge(s_bc, 2 * n + half + 1)
                        nc.vector.tensor_tensor(ln_t[:, d % 2, :], psum[:, 6 + half, 0:HALF], xres[:, d, cols_of(half)],
                                                ALU.add).then_inc(s_t, 1)
                    for d in (a, a + 1):
                        dve.wait_ge(s_t, k + d + 1)
                        nc.vector.tensor_tensor(ln_t[:, d % 2, :], ln_t[:, d % 2, :], psum[:, 6 + half, HALF:],
                                                ALU.mult).then_inc(s_tn, 1)
                    if n + 1 < NLAYERS:
                        for d in (a, a + 1):
                            dve.wait_ge(s_tn, k + d + 1)
                            low_x(n + 1, half, d, ln_t[:, d % 2, :])

            def layer_norm(n):
                lead = [u for u in range(FIRST[n + 1] + 4 - tail_units(n), FIRST[n + 1] + 4) if u < lead_limit(n)]
                last = FIRST[n + 1] - tail(n)
                z_tail(n, 0, last)
                if n == 0:
                    mod_column(ada_chunks(n) + NF // 2 + 2)
                ln_moments(n, 0)
                if tail_units(n) == 3 and lead:
                    low(lead.pop(0))
                ln_inverse(n, 0)
                ln_tiles(n, 0, (0, 1))
                if lead:
                    low(lead.pop(0))
                z_tail(n, 1, last)
                ln_tiles(n, 0, (2, 3))
                if lead:
                    low(lead.pop(0))
                ln_moments(n, 1)
                ln_inverse(n, 1)
                ln_tiles(n, 0, range(4, KD))
                ln_tiles(n, 1, range(KD))

            def ffn(n):
                u0, h0, c0 = FIRST[n], NF * ffn_index[n], ada_chunks(n)
                dve.wait_ge(s_x, 2 * (n + 1) * KD)

                def in_round(i, start, with_ada):
                    for j in range(2):
                        f = at(2 * start + j, 2, i)
                        u = at(u0 + 4 * start + 2 * j, 4, i)
                        wait(dve, s_sg, f + (h0 + 1))
                        wait(dve, s_unit, u + 2)
                        nc.vector.tensor_tensor(duo[:, j, :], duo[:, j, :], psum[:, 2 * j + 1, :],
                                                ALU.mult).then_inc(s_gu, 1)
                        low(u + 4)
                        wait(dve, s_hh, f + (h0 + 1))
                        wait(dve, s_gu, f + (START + h0 + 1))
                        nc.vector.tensor_tensor(hl[:, one(f), :], duo[:, j:j + 1, :],
                                                hh[:, one(f), :].bitcast(F32), ALU.subtract).then_inc(s_hl, 1)
                        low(u + 5)
                        if with_ada and j == 0:
                            if start:
                                mod_column(at(c0 + start - 1, 1, i))
                            ada(at(c0 + start, 1, i))

                if ada_rounds(n):
                    in_round(None, 0, True)
                    with dve.Fori(0, ada_rounds(n) - 1) as i:
                        in_round(i, 1, True)
                if ada_rounds(n) < NF // 2:
                    with dve.Fori(0, NF // 2 - ada_rounds(n)) as i:
                        in_round(i, ada_rounds(n), False)
                derive(n, 0.5)
                clear_sums(n)

                for d in range(d0(n)):
                    u = u0 + 2 * NF + 3 * d
                    low(u + 4)
                    low(u + 5)
                    z_tile(n, d, 4 + d % 2, u + 2)
                    if u + 6 < lead_limit(n):
                        low(u + 6)
                    if d == 0 and ada_rounds(n):
                        mod_column(c0 + ada_rounds(n) - 1)
                    if n == 0:
                        if d in (1, 4):
                            mod_column(c0 + NF // 2 + d // 4)
                        ada(*ada_share(c0, d))
                layer_norm(n)

            def gates():
                steps = [0]

                def step(ins):
                    steps[0] += 1
                    ins.then_inc(s_gr, 1)

                dve.wait_ge(s_gp, 1)
                dve.wait_ge(s_gb, 32)
                step(nc.vector.tensor_scalar(grow[:, 0, :], psum[0:HEADS, 6, :], gbias[:, 0:1], None, ALU.add))
                step(nc.vector.tensor_copy(grow[:, 1, :], psum[32:32 + HEADS, 6, :]))
                dve.wait_ge(s_gr, 2)
                step(nc.vector.tensor_scalar(grow[:, 1, :], grow[:, 1, :], gbias[:, 1:2], None, ALU.add))
                dve.wait_ge(s_gr, 3)
                step(nc.vector.tensor_scalar(grow[:, 3, :], grow[:, 1, :], 0.0, None, ALU.min))
                step(nc.vector.memset(grow[:, 4, :], 0.0))
                dve.wait_ge(s_ga, 3)
                dve.wait_ge(s_gr, 5)
                step(nc.vector.tensor_tensor(grow[:, 3, :], grow[:, 3, :], grow[:, 2, :], ALU.subtract))
                dve.wait_ge(s_gr, 6)
                step(nc.vector.tensor_tensor_scan(grow[:, 5, :], grow[:, 3, :], grow[:, 0, :], 0.0,
                                                  ALU.add, ALU.max))
                for b in range(NB):
                    step(nc.vector.tensor_tensor_scan(decay[:, SEG[b]:SEG[b + 1]], grow[:, 3, b * P:],
                                                      grow[:, 4, b * P:], 0.0, ALU.add, ALU.add))
                dve.wait_ge(s_gr, 7 + NB)
                for b in range(NB):
                    step(nc.vector.tensor_tensor(grow[:, 6, b * P:(b + 1) * P], grow[:, 0, b * P:(b + 1) * P],
                                                 decay[:, SEG[b]:SEG[b] + P], ALU.subtract))
                dve.wait_ge(s_gr, 7 + 2 * NB)
                for b in range(NB):
                    step(nc.vector.tensor_tensor(decay[:, SEG[b]:SEG[b + 1]], decay[:, SEG[b]:SEG[b + 1]],
                                                 grow[:, 5, b * P:], ALU.subtract))
                assert steps[0] == GATE_ROW_STEPS

            def mlstm():
                n, u0 = 1, FIRST[1]
                dve.wait_ge(s_x, 2 * (n + 1) * KD)
                dve.wait_ge(s_ghi, 1)
                nc.vector.tensor_tensor(g_lo[:, :, :], g_raw[:, :, :], g_hi[:, :, :].bitcast(F32),
                                        ALU.subtract).then_inc(s_glo, 1)
                for half in range(2):
                    for j in range(4):
                        m, s = 4 * half + j, j % 2
                        dve.wait_ge(s_ev, ev_before(1) + m + 1)
                        dve.wait_ge(s_qk, m + START - 1)
                        tap = lambda k: cols[:, 1, 72 + KD * k + m:73 + KD * k + m]
                        nc.vector.tensor_scalar(conv[:, s, :], duo[:, s, :], tap(3), None, ALU.mult).then_inc(s_cx, 1)
                        for k in (1, 2, 3):
                            dve.wait_ge(s_cx, m * 3 + k)
                            nc.vector.scalar_tensor_tensor(out=conv[:, s, k:], in0=duo[:, s, :SEQ - k],
                                                           scalar=tap(3 - k), in1=conv[:, s, k:],
                                                           op0=ALU.mult, op1=ALU.add
                                                           ).then_inc(s_cf if k == 3 else s_cx, 1)
                        low(u0 + m + 4)
                    if half == 0:
                        gates()
                dve.wait_ge(s_cT, 1)
                nc.vector.tensor_copy(ccol[:, :, :], psum[:, 6, 0:NB * HEADS].rearrange("p (b h) -> p b h", h=HEADS)
                                      ).then_inc(s_cc, 1)
                with dve.Fori(0, 2) as i:
                    for j in range(4):
                        m = Pos(j, 4, i)
                        low(m + (u0 + KD + 4))
                        wait(dve, s_vt, m + (START + 1))
                        nc.vector.tensor_copy(vtok[:, :, bass.ds((m * P).at, P)],
                                              psum[:, 4 + j % 2, :].rearrange("p (b q) -> p b q", q=P)
                                              ).then_inc(s_vc, 1)
                derive(n, 1.0)

                def weigh(h):
                    dve.wait_ge(s_S, h + 1)
                    dve.wait_ge(s_dm, 4 * (h + 1))
                    for bank, lo, hi in ((0, SEG[0], SEG[1]), (1, SEG[1], SEG[2]), (2, SEG[2], SEG[4])):
                        nc.vector.scalar_tensor_tensor(out=dmat[:, h % 2, lo:hi], in0=psum[:, bank, 0:hi - lo],
                                                       scalar=DQK ** -0.5, in1=dmat[:, h % 2, lo:hi],
                                                       op0=ALU.mult, op1=ALU.mult).then_inc(s_SD, 1)

                clear_sums(n)
                low(u0 + 2 * KD + 4)
                weigh(0)
                low(u0 + 2 * KD + 5)
                for h in range(HEADS):
                    s = h % 2
                    dve.wait_ge(s_ab, h + 1)
                    nc.vector.tensor_tensor(den[:, s, :], den[:, s, :], drow[:, s, SEG[NB]:], ALU.max
                                            ).then_inc(s_dd, 1)
                    if h + 1 < HEADS:
                        weigh(h + 1)
                    if h + 2 < HEADS - 1:
                        low(u0 + 2 * KD + h + 6)
                    dve.wait_ge(s_dsq, h + 1)
                    dve.wait_ge(s_ms, h + 1)
                    nc.vector.scalar_tensor_tensor(out=den[:, s, :], in0=psum[:, 7, :], scalar=1 / P,
                                                   in1=den[:, s, :], op0=ALU.mult, op1=ALU.add).then_inc(s_tt, 1)
                    dve.wait_ge(s_sdm, h + 1)
                    nc.vector.reciprocal(den[:, s, :], den[:, s, :]).then_inc(s_rr, 1)
                    dve.wait_ge(s_rr, h + 1)
                    nc.vector.tensor_tensor(y_of(h), psum[:, 3 + s, :], den[:, s, :], ALU.mult).then_inc(s_y1, 1)

                def gate(h):
                    dve.wait_ge(s_y1, h + 1)
                    dve.wait_ge(s_og, h + 1)
                    nc.vector.scalar_tensor_tensor(out=y_of(h), in0=y_of(h), scalar=cols[:, 0, 104 + h:105 + h],
                                                   in1=sig[:, h, :], op0=ALU.mult, op1=ALU.mult).then_inc(s_y2, 1)

                gate(0)
                for h in range(HEADS):
                    if h + 1 < HEADS:
                        gate(h + 1)
                    dve.wait_ge(s_y2, h + 1)
                    dve.wait_ge(s_yh, h + 1)
                    nc.vector.tensor_tensor(xl[:, h, :], y_of(h), xh[:, h, :].bitcast(F32),
                                            ALU.subtract).then_inc(s_yr, 1)
                    if h == 1:
                        low(u0 + 3 * KD + 3)
                for d in range(d0(n)):
                    low(u0 + 3 * KD + 4 + d)
                    z_tile(n, d, d, u0 + 3 * KD + d)
                layer_norm(n)

            def attention():
                n = 4
                dve.wait_ge(s_x, 2 * (n + 1) * KD)

                def head(t, prev):
                    for j in range(9):
                        m = t * 9 + j
                        low(m + (ATT0 + ATT_RING))
                        if prev is not None:
                            if j == 0:
                                v_tokens(prev, 2)
                                class_stats(prev)
                            if j == 2:
                                token_stats(prev)
                            if j == 3:
                                scale_prob(prev)
                            if j == 4:
                                prob_out(prev)
                            if j == 5:
                                out_join(prev)
                            if j == 6:
                                out_low(prev)
                        if j == 6:
                            mask_scores(t)
                        if j == 7:
                            v_tokens(t, 0)
                        if j == 8:
                            v_tokens(t, 1)

                def v_tokens(t, g):
                    wait(dve, s_vt, t * 3 + (START + KD + g + 1))
                    nc.vector.tensor_copy(vt[:, g, :, :], psum[:, 7, :].rearrange("p (b q) -> p b q", q=P)
                                          ).then_inc(s_vc, 1)

                def mask_scores(t):
                    wait(dve, s_as, t + 1)
                    own = lambda n_b: mask[:, 1:2, :].broadcast_to([P, n_b, P])

                    def masked(lo, n_b, bank, col, m):
                        nc.vector.tensor_tensor(prob[:, lo:lo + n_b, :],
                                                psum[:, bank, col * P:(col + n_b) * P].rearrange(
                                                    "p (b q) -> p b q", q=P), m, ALU.add).then_inc(s_am, 1)

                    masked(0, 1, 3, 0, own(1))
                    masked(1, 2, 3, 1, mask[:, 0:2, :])
                    masked(3, 2, 4, 0, mask[:, 0:2, :])
                    masked(5, 2, 4, 2, mask[:, 0:2, :])
                    masked(7, 4, 5, 0, own(4))
                    masked(11, 4, 6, 0, mask[:, 2:3, :].broadcast_to([P, 4, P]))
                    wait(dve, s_am, t * 6 + 6)
                    nc.vector.tensor_reduce(mx[:, 0, 0:1], prob[:, 0, :], AX.X, ALU.max).then_inc(s_mxr, 1)
                    nc.vector.tensor_reduce(mx[:, 0, 1:4], prob[:, 1:7, :].rearrange("p (b c) q -> p b (c q)", c=2),
                                            AX.X, ALU.max).then_inc(s_mxr, 1)
                    nc.vector.tensor_reduce(mx[:, 1:3, :].rearrange("p g b -> p (g b)"), prob[:, 7:15, :],
                                            AX.X, ALU.max).then_inc(s_mxr, 1)
                    wait(dve, s_mxr, t * 3 + 3)
                    nc.vector.tensor_scalar(nb[:, :, :], mx[:, :, :], -SCALE, None, ALU.mult).then_inc(s_nb, 1)

                def class_stats(t):
                    nc.vector.tensor_tensor(pm[:, 0, :], mx[:, 1, :], mx[:, 2, :], ALU.max).then_inc(s_pc, 1)
                    wait(dve, s_pc, t * 6 + 1)
                    for g in range(2):
                        nc.vector.tensor_tensor(pd[:, g, :], mx[:, 1 + g, :], pm[:, 0, :], ALU.subtract
                                                ).then_inc(s_pc, 1)
                    wait(dve, s_pe, t + 1)
                    wait(dve, s_ae, t * 12 + 12)
                    for g in range(2):
                        nc.vector.tensor_tensor(pd[:, g, :], pe12[:, g, :], dn[:, 1 + g, :], ALU.mult
                                                ).then_inc(s_pc, 1)
                    wait(dve, s_pc, t * 6 + 5)
                    nc.vector.tensor_tensor(pm[:, 1, :], pd[:, 0, :], pd[:, 1, :], ALU.add).then_inc(s_pc, 1)

                def token_stats(t):
                    wait(dve, s_pld, t * 16 + 16)
                    nc.vector.tensor_tensor(nd[:, 0, :], mx[:, 0, :], nm[:, 0, :], ALU.max).then_inc(s_nc, 1)
                    wait(dve, s_nc, t * 8 + 1)
                    nc.vector.tensor_tensor(nj[:, 0, :], mx[:, 0, :], nd[:, 0, :], ALU.subtract).then_inc(s_nc, 1)
                    nc.vector.tensor_tensor(nj[:, 1, :], nm[:, 0, :], nd[:, 0, :], ALU.subtract).then_inc(s_nc, 1)
                    wait(dve, s_ne, t + 1)
                    nc.vector.tensor_tensor(nd[:, 0, :], dn[:, 0, :], ne[:, 0, :], ALU.mult).then_inc(s_nc, 1)
                    nc.vector.tensor_tensor(nd[:, 1, :], nm[:, 1, :], ne[:, 1, :], ALU.mult).then_inc(s_nc, 1)
                    wait(dve, s_nc, t * 8 + 5)
                    nc.vector.tensor_tensor(nd[:, 0, :], nd[:, 0, :], nd[:, 1, :], ALU.add).then_inc(s_nc, 1)
                    wait(dve, s_nc, t * 8 + 6)
                    nc.vector.reciprocal(nd[:, 1, :], nd[:, 0, :]).then_inc(s_nc, 1)
                    wait(dve, s_nc, t * 8 + 7)
                    nc.vector.tensor_tensor(f12[:, :], ne[:, 1, :], nd[:, 1, :], ALU.mult).then_inc(s_nc, 1)
                    nc.vector.tensor_tensor(fac[:, 0, :], ne[:, 0, :], nd[:, 1, :], ALU.mult).then_inc(s_fac, 1)

                def scale_prob(t):
                    wait(dve, s_nld, t * 16 + 16)
                    for g in range(2):
                        nc.vector.tensor_tensor(fac[:, 1 + g, :], pe12[:, g, :], pf[:, :], ALU.mult
                                                ).then_inc(s_fac, 1)
                    wait(dve, s_fac, t * 3 + 3)

                    def scaled(blk, f, shape):
                        nc.vector.tensor_tensor(blk, blk, f.unsqueeze(2).broadcast_to(shape), ALU.mult
                                                ).then_inc(s_sc, 1)

                    scaled(prob[:, 0:1, :], fac[:, 0, 0:1], [P, 1, P])
                    scaled(prob[:, 1:7, :].rearrange("p (b c) q -> p b (c q)", c=2), fac[:, 0, 1:4], [P, 3, 2 * P])
                    scaled(prob[:, 7:15, :], fac[:, 1:3, :].rearrange("p g b -> p (g b)"), [P, 8, P])

                def prob_out(t):
                    wait(dve, s_pt, t + 1)
                    nc.vector.tensor_copy(probT[:, 4:8, :].rearrange("p b q -> p (b q)"), psum[:, 4, :]).then_inc(s_ptd, 1)
                    nc.vector.tensor_copy(probT[:, 12:15, :].rearrange("p b q -> p (b q)"), psum[:, 6, 0:3 * P]
                                          ).then_inc(s_ptd, 1)

                def out_join(t):
                    wait(dve, s_on, t + 1)
                    y = yn[:, :].rearrange("p (i r) -> p i r", r=DIL)
                    nc.vector.tensor_tensor(y, y, psum[:, 3, :].rearrange("p (r i) -> p i r", r=DIL), ALU.add
                                            ).then_inc(s_oe, 1)

                def out_low(t):
                    wait(dve, s_yh, t + (HEADS + 1))
                    nc.vector.tensor_tensor(yl[:, one(t), :], yn[:, :].unsqueeze(1),
                                            yh[:, one(t), :].bitcast(F32), ALU.subtract).then_inc(s_yr, 1)

                head(Pos(0), None)
                with dve.Fori(0, HEADS - 1) as i:
                    head(Pos(1, 1, i), Pos(0, 1, i))
                t = Pos(HEADS - 1)
                v_tokens(t, 2)
                class_stats(t)
                derive(n, 1.0)
                low(ATT1 + ATT_RING)
                token_stats(t)
                clear_sums(n)
                scale_prob(t)
                prob_out(t)
                out_join(t)
                out_low(t)
                for d in range(d0(n)):
                    low(ATT1 + 4 + d)
                    z_tile(n, d, d, ATT1 + d)
                layer_norm(n)

            for k, (s, count) in enumerate(((s_z, START), (s_gu, START), (s_hl, START), (s_ev, EV_START), (s_cf, START),
                             (s_vt, START), (s_vc, START), (s_qk, START))):
                nc.vector.memset(token[:, k:k + 1], 0.0).then_inc(s, count)
            dve.wait_ge(s_colsT, 1)
            nc.vector.tensor_copy(cols[:, 0, 0:112], psum[:, 4, 0:112]).then_inc(s_cols, 1)
            dve.wait_ge(s_colsT, 3)
            nc.vector.tensor_copy(cols[:, 1, 0:104], psum[:, 5, 0:104]).then_inc(s_cols, 1)
            nc.vector.tensor_copy(cols[:, 2, 0:72], psum[:, 6, 0:72]).then_inc(s_cols, 1)
            dve.wait_ge(s_const, 7)
            nc.vector.tensor_reduce(sel4[:, :], ident[:, :].rearrange("p (a b) -> p b a", b=DIL), AX.X, ALU.add
                                    ).then_inc(s_mask, 1)
            dve.wait_ge(s_mask, 1)
            nc.vector.tensor_scalar(sel4[:, :], sel4[:, :], -MASKED, MASKED, ALU.mult, ALU.add).then_inc(s_mask, 1)
            dve.wait_ge(s_mask, 2)
            nc.vector.tensor_tensor(mask[:, 2, :].rearrange("p (a b) -> p a b", b=DIL),
                                    mask[:, 1, :].rearrange("p (a b) -> p a b", b=DIL),
                                    sel4[:, :].unsqueeze(1).broadcast_to([P, P // DIL, DIL]), ALU.add
                                    ).then_inc(s_mask, 1)
            dve.wait_ge(s_cond, 1)
            total = ada_first[:, 0, :]
            for k in range(KD):
                if k == 6:
                    for u in range(RING):
                        low(u)
                dve.wait_ge(s_first[k], 16)
                if k == 0:
                    nc.vector.tensor_scalar(total, total, cond[:, 0:1], None, ALU.mult).then_inc(s_ada, UPFRONT)
                    continue
                dve.wait_ge(s_ada, UPFRONT * k)
                for a in range(2 if k == KD - 1 else 1):
                    c = slice(0, UPFRONT * CHUNK) if k < KD - 1 else slice(a * KD * P, (a + 1) * KD * P)
                    nc.vector.scalar_tensor_tensor(out=total[:, c], in0=ada_first[:, k, c], scalar=cond[:, k:k + 1],
                                                   in1=total[:, c], op0=ALU.mult, op1=ALU.add
                                                   ).then_inc(s_ada, UPFRONT if k < KD - 1 else UPFRONT // 2)
            dve.wait_ge(s_modp, UPFRONT)
            nc.vector.tensor_tensor(mod[:, 0:2 * KD], psum[:, 7, 0:2 * KD], cols[:, 1, 0:2 * KD], ALU.add
                                    ).then_inc(s_mod, UPFRONT)
            dve.wait_ge(s_mod, UPFRONT)
            nc.vector.tensor_scalar(mul_c[:, 0:KD], mod[:, KD:2 * KD], 1.0, None, ALU.add).then_inc(s_der, 1)
            nc.vector.tensor_copy(add_c[:, 0:KD], mod[:, 0:KD]).then_inc(s_der, 1)
            dve.wait_ge(s_der, 2)
            for half, d in [(h, d) for h in range(2) for d in range(KD)]:
                dve.wait_ge(s_xnew, d + 1)
                if d >= 2 or half:
                    dve.wait_ge(s_x, KD * half + d - 1)
                low_x(0, half, d, xres[:, d, cols_of(half)])
            ffn(0)
            mlstm()
            ffn(2)
            ffn(3)
            attention()
            ffn(5)
            for b in range(NB):
                dve.wait_ge(s_fT, 2 * b + 2)
                nc.vector.tensor_copy(xtok[:, b, SEQ:], psum[:, 2 * b + 1, :]).then_inc(s_fo2, 1)

        @block.tensor
        def _(pe):
            def products(u, k, out_ap, rh, rl, start, stop):
                s = slot_of(u)
                for w, r, first, last in ((w_hi, rh, True, False), (w_hi, rl, False, False), (w_lo, rh, False, True)):
                    mm = nc.tensor.matmul(out_ap, w[:, s, k, :], r, start=start and first, stop=stop and last)
                return mm

            def strip(u, bank, kts=KD, rh=xh, rl=xl, k0=0, start=True, stop=True):
                wait(pe, s_lo, pos(u) + 1)
                for k in range(kts):
                    mm = products(u, k, psum[:, bank, :], rh[:, k0 + k, :], rl[:, k0 + k, :],
                                  start and k == 0, stop and k == kts - 1)
                mm.then_inc(s_unit, 1)

            def first_strips(n, count):
                for half in range(2):
                    c = cols_of(half)
                    for k in range(KD):
                        pe.wait_ge(s_x, 2 * KD * n + KD * half + k + 1)
                        for j in range(count):
                            joins = half == 0 and k == JOIN[j]
                            if half == 0 and k < JOIN[j]:
                                continue
                            if joins:
                                pe.wait_ge(s_lo, FIRST[n] + j + 1)
                            for kk in range(k + 1) if joins else (k,):
                                mm = products(FIRST[n] + j, kk, psum[:, j, c], xh[:, kk, c], xl[:, kk, c],
                                              kk == 0, kk == KD - 1)
                            if half and k == KD - 1:
                                mm.then_inc(s_unit, 1)
                        if half == 0 and n > 0:
                            if k == 1:
                                sums(n - 1, 1)
                            if k == 3:
                                spread(n - 1, 1)

            def halves(n, first_unit, rh, rl):
                units = [(i, q) for i in range(tail(n)) for q in range(tail_units(n) // tail(n))]
                per = len(units) // tail(n)
                for half in range(2):
                    c = cols_of(half)
                    for a, (i, q) in enumerate(units):
                        k0, kt = K_CHUNKS[q] if n in ffn_index else (0, KD)
                        bank = tail_bank(n, half, i)
                        if half == 0:
                            pe.wait_ge(s_lo, first_unit + a + 1)
                        if q == 0:
                            read = d0(n) + i - 1 if half == 0 else d0(n) + (0 if n in ffn_index else i + 1)
                            pe.wait_ge(s_z, z_before(n) + read)
                        for k in range(kt):
                            mm = products(first_unit + a, k, psum[:, bank, c], rh[:, k0 + k, c], rl[:, k0 + k, c],
                                          q == 0 and k == 0, q == per - 1 and k == kt - 1)
                        if half:
                            mm.then_inc(s_unit, 1)
                        elif q == per - 1:
                            mm.then_inc(s_tail, 1)
                        if half and a == 0:
                            sums(n, 0)
                        if half and a == 1:
                            spread(n, 0)
                    if half == 0 and n == 0:
                        mod_sum(ada_chunks(n) + NF // 2 + 2)

            def mod_sum(ch):
                wait(pe, s_ada, pos(ch) * KD + KD)
                for j in range(4):
                    mm = nc.tensor.matmul(psum[:, 7, j:j + 1], ada_acc[:, j * P:(j + 1) * P], ones[:, 0:1],
                                          start=True, stop=True)
                mm.then_inc(s_modp, 1)

            def sums(n, half):
                done = acc_before(n) + 1 + d0(n) + (tail(n) - 1) * (half + 1)
                pe.wait_ge(s_acc1, done)
                pe.wait_ge(s_acc2, done)
                pe.wait_ge(s_z, z_before(n) + d0(n) + tail(n) * (half + 1))
                pe.wait_ge(s_sq, sq_before(n) + d0(n) + tail(n) * (half + 1))
                if half and ada_rounds(n):
                    pe.wait_ge(s_mod, ada_chunks(n + 1))
                for a, last in ((0, xres[:, KD - 1, :]), (1, sq)):
                    for b in range(2):
                        t = slice((2 * half + b) * P, (2 * half + b + 1) * P)
                        dst = psum[:, 6 + half, 2 * a + b:2 * a + b + 1]
                        nc.tensor.matmul(dst, acc[:, a, t], ones[:, 0:1], start=True, stop=False)
                        mm = nc.tensor.matmul(dst, last[:, t], ones[:, 0:1], start=False, stop=True)
                mm.then_inc(s_stat, 1)

            def spread(n, half):
                pe.wait_ge(s_rstd, 2 * n + half + 1)
                for a, q in enumerate((0, 4)):
                    for b in range(2):
                        mm = nc.tensor.matmul(psum[:, 6 + half, (2 * a + b) * P:(2 * a + b + 1) * P],
                                              st[:, half, q, b:b + 1].broadcast_to([P, P]), ident[:, :],
                                              start=True, stop=True)
                mm.then_inc(s_bc, 1)

            def ffn(n):
                u0, h0, c0 = FIRST[n], START + NF * ffn_index[n], ada_chunks(n)
                pe.wait_ge(s_gu, h0)
                first_strips(n, RING)

                def in_round(i, start, with_ada):
                    for j in range(2):
                        wait(pe, s_gu, Pos(h0 + 2 * start + j + 1, 2, i))
                        strip(Pos(u0 + 4 * start + 4 + 2 * j, 4, i), 2 * j)
                        strip(Pos(u0 + 4 * start + 5 + 2 * j, 4, i), 2 * j + 1)
                        if with_ada and j == 0:
                            mod_sum(Pos(c0 + start, 1, i))

                r = min(ada_rounds(n), NF // 2 - 1)
                if r:
                    with pe.Fori(0, r) as i:
                        in_round(i, 0, True)
                if r < NF // 2 - 1:
                    with pe.Fori(0, NF // 2 - 1 - r) as i:
                        in_round(i, r, False)
                for d in range(d0(n)):
                    pe.wait_ge(s_z, z_before(n) + d - 1)
                    for q, (k0, kt) in enumerate(K_CHUNKS):
                        if d == 0:
                            pe.wait_ge(s_hl, h0 + k0 + kt)
                        strip(u0 + 2 * NF + 3 * d + q, 4 + d % 2, kt, hh, hl, k0, q == 0, q == 2)
                    if d == 0 and ada_rounds(n) == NF // 2:
                        mod_sum(c0 + NF // 2 - 1)
                    if n == 0 and d in (1, 4):
                        mod_sum(c0 + NF // 2 + d // 4)
                halves(n, u0 + 2 * NF + 3 * d0(n), hh, hl)

            def mlstm():
                n, u0, e0 = 1, FIRST[1], ev_before(1)
                first_strips(n, RING)
                pe.wait_ge(s_glo, 1)
                for k in range(KD):
                    for w, r, first, last in ((g_hi, xh, k == 0, False), (g_hi, xl, False, False),
                                              (g_lo, xh, False, k == KD - 1)):
                        mm = nc.tensor.matmul(psum[:, 6, :], w[:, k, :], r[:, k, :], start=first, stop=last)
                mm.then_inc(s_gp, 1)
                for j in range(4):
                    pe.wait_ge(s_ev, e0 + j + 1)
                    strip(u0 + 4 + j, j)
                pe.wait_ge(s_gr, 7 + 2 * NB)
                for b in range(NB):
                    mm = nc.tensor.transpose(psum[:, 6, b * HEADS:(b + 1) * HEADS],
                                             grow[:, 6, b * P:(b + 1) * P], ident[0:HEADS, 0:HEADS])
                mm.then_inc(s_cT, 1)
                with pe.Fori(0, 2) as i:
                    def turn(j):
                        h = Pos(j, 4, i)
                        wait(pe, s_ev, h + (e0 + KD + 1))
                        wait(pe, s_vc, h + (START - 1))
                        for b in range(NB):
                            mm = nc.tensor.transpose(psum[:, 4 + j % 2, b * P:(b + 1) * P],
                                                     duo[:, j % 2, b * P:(b + 1) * P], ident[:, :])
                        mm.then_inc(s_vt, 1)
                    for j in range(4):
                        m = Pos(KD + j, 4, i)
                        wait(pe, s_ev, m + (e0 - 3))
                        strip(m + u0, j)
                        if j >= 1:
                            turn(j - 1)
                    turn(3)

                def gate_strip(h):
                    if h == 0:
                        pe.wait_ge(s_cc, 1)
                    else:
                        pe.wait_ge(s_ev, e0 + 2 * KD + h)
                    strip(u0 + 2 * KD + h, 6)

                def scores(h):
                    a, o = h // 2, DQK * (h % 2)
                    if h >= 1:
                        pe.wait_ge(s_SD, 3 * h)
                    for b in range(NB):
                        bank, col = ((0, 0), (1, 0), (2, 0), (2, 2 * P))[b]
                        mm = nc.tensor.matmul(psum[:, bank, col:col + SEQ - b * P],
                                              qk[o:o + DQK, HEADS // 2 + a, b * P:(b + 1) * P],
                                              qk[o:o + DQK, a, b * P:], start=True, stop=True)
                    mm.then_inc(s_S, 1)

                pe.wait_ge(s_qk, START + KD)
                pe.wait_ge(s_vc, START + KD)
                gate_strip(0)
                scores(0)
                gate_strip(1)
                for h in range(HEADS):
                    s = h % 2
                    pe.wait_ge(s_SD, 3 * (h + 1))
                    if h >= 2:
                        pe.wait_ge(s_y1, h - 1)
                    for b in range(NB):
                        nc.tensor.matmul(psum[:, 3 + s, b * P:], vtok[:, b, h * P:(h + 1) * P],
                                         dmat[:, s, SEG[b]:SEG[b + 1]], start=(b == 0), stop=(b == NB - 1))
                    if h >= 1:
                        pe.wait_ge(s_ab, h)
                    for b in range(NB):
                        mm = nc.tensor.matmul(psum[:, 5, b * P:], ones[:, :], dmat[:, s, SEG[b]:SEG[b + 1]],
                                              start=(b == 0), stop=(b == NB - 1))
                    mm.then_inc(s_nd, 1)
                    if h + 1 < HEADS:
                        scores(h + 1)
                    if h + 2 < HEADS - 1:
                        gate_strip(h + 2)
                    pe.wait_ge(s_nsq, h + 1)
                    if h >= 1:
                        pe.wait_ge(s_tt, h)
                    nc.tensor.matmul(psum[:, 7, :], ones[:, :], nsq[:, :], start=True, stop=True).then_inc(s_ms, 1)
                gate_strip(HEADS - 1)
                pe.wait_ge(s_y1, HEADS)
                for k in range(HEADS):
                    pe.wait_ge(s_yr, k + 1)
                    for d in range(4):
                        start = 2 if d == 3 else 0
                        if k < start:
                            continue
                        if k == start:
                            pe.wait_ge(s_lo, u0 + 3 * KD + d + 1)
                        for kk in range(k + 1) if k == start else (k,):
                            mm = products(u0 + 3 * KD + d, kk, psum[:, d, :], xh[:, kk, :], xl[:, kk, :],
                                          kk == 0, kk == HEADS - 1)
                        if k == HEADS - 1:
                            mm.then_inc(s_unit, 1)
                for d in range(4, d0(n)):
                    strip(u0 + 3 * KD + d, d)
                halves(n, u0 + 3 * KD + d0(n), xh, xl)

            def attention():
                n, e0 = 4, ev_before(4)

                def head(t, prev):
                    for j in range(9):
                        m = t * 9 + j
                        if prev is not None or j >= ATT_RING:
                            wait(pe, s_ev, m + (e0 - 2))
                            strip(m + ATT0, j % 3)
                        if prev is not None:
                            if j == 0:
                                turn(prev, 2)
                            if j == 4:
                                prob_turn(prev)
                            if j == 5:
                                values(prev)
                        if j == 6:
                            scores(t)
                        if j == 7:
                            turn(t, 0)
                        if j == 8:
                            turn(t, 1)

                def turn(t, g):
                    wait(pe, s_ev, t * 9 + (e0 + 7 + g))
                    wait(pe, s_vc, t * 3 + (START + KD + g))
                    if g == 0:
                        wait(pe, s_on, t)
                    for b in range(NB):
                        mm = nc.tensor.transpose(psum[:, 7, b * P:(b + 1) * P], duo[:, g % 2, b * P:(b + 1) * P],
                                                 ident[:, :])
                    mm.then_inc(s_vt, 1)

                def scores(t):
                    wait(pe, s_ev, t * 9 + (e0 + 6))
                    wait(pe, s_oe, t)
                    for b in range(NB):
                        lo = max(b - 1, 0)
                        bank, col = ((3, 0), (3, 1), (4, 0), (4, 2))[b]
                        nc.tensor.matmul(psum[:, bank, col * P:(col + b + 1 - lo) * P],
                                         qT[:, 0, b * P:(b + 1) * P], kT[:, 0, lo * P:(b + 1) * P],
                                         start=True, stop=True)
                    for g in (1, 2):
                        for b in range(NB):
                            mm = nc.tensor.matmul(psum[:, 4 + g, b * P:(b + 1) * P], qT[:, g, b * P:(b + 1) * P],
                                                  kT[:, g, b * P:(b + 1) * P], start=True, stop=True)
                    mm.then_inc(s_as, 1)

                def prob_turn(t):
                    wait(pe, s_sc, t * 3 + 3)
                    for b in range(ATT_BLOCKS):
                        mm = nc.tensor.transpose(psum[:, 3 + b // 4, (b % 4) * P:(b % 4 + 1) * P], prob[:, b, :],
                                                 ident[:, :])
                    mm.then_inc(s_pt, 1)

                def values(t):
                    wait(pe, s_pta, t * 2 + 2)
                    wait(pe, s_ptd, t * 2 + 2)
                    wait(pe, s_vc, t * 3 + (START + KD + 3))
                    for b in range(NB):
                        dst = psum[:, 7, b * P:(b + 1) * P]
                        if b:
                            nc.tensor.matmul(dst, vt[:, 0, b - 1, :], probT[:, 2 * b - 1, :], start=True, stop=False)
                        nc.tensor.matmul(dst, vt[:, 0, b, :], probT[:, 2 * b, :], start=(b == 0), stop=True)
                    for b in range(NB):
                        dst = psum[:, 3, b * P:(b + 1) * P]
                        nc.tensor.matmul(dst, vt[:, 1, b, :], probT[:, 7 + b, :], start=True, stop=False)
                        mm = nc.tensor.matmul(dst, vt[:, 2, b, :], probT[:, 11 + b, :], start=False, stop=True)
                    mm.then_inc(s_o, 1)

                first_strips(n, ATT_RING)
                head(Pos(0), None)
                with pe.Fori(0, HEADS - 1) as i:
                    head(Pos(1, 1, i), Pos(0, 1, i))
                t = Pos(HEADS - 1)
                turn(t, 2)
                pe.wait_ge(s_ev, e0 + ATT_HEAD_UNITS)
                pe.wait_ge(s_lo, ATT1 + 3)
                for k in range(HEADS - 1):
                    pe.wait_ge(s_yr, HEADS + k + 1)
                    for d in range(3):
                        products(ATT1 + d, k, psum[:, d, :], yh[:, k, :], yl[:, k, :], k == 0, False)
                prob_turn(t)
                values(t)
                pe.wait_ge(s_yr, 2 * HEADS)
                for d in range(3):
                    products(ATT1 + d, HEADS - 1, psum[:, d, :], yh[:, HEADS - 1, :], yl[:, HEADS - 1, :],
                             False, True).then_inc(s_unit, 1)
                for d in range(3, d0(n)):
                    strip(ATT1 + d, d, KD, yh, yl)
                halves(n, ATT1 + d0(n), yh, yl)

            pe.wait_ge(s_const, 5)
            pe.wait_ge(s_rows[0], 16 * 4)
            for a, rows in enumerate((112, 104, 72)):
                if a == 1:
                    pe.wait_ge(s_rows[1], 16 * 3)
                nc.tensor.transpose(psum[:, 4 + a, 0:rows], rows_t[0:rows, a, :], ident[0:rows, 0:rows]
                                    ).then_inc(s_colsT, 1)
            pe.wait_ge(s_xtok, 16)
            for d in range(KD):
                if d >= 4:
                    pe.wait_ge(s_xnew, d - 3)
                for b in range(NB):
                    mm = nc.tensor.transpose(psum[:, d % 4, b * P:(b + 1) * P], xtok[:, b, d * P:(d + 1) * P],
                                             ident[:, :])
                mm.then_inc(s_xT, 1)
            for j in range(2 * KD):
                if j % KD == 0:
                    pe.wait_ge(s_ada, UPFRONT * KD - (UPFRONT // 2 if j == 0 else 0))
                mm = nc.tensor.matmul(psum[:, 7, j:j + 1], ada_first[:, 0, j * P:(j + 1) * P], ones[:, 0:1],
                                      start=True, stop=True)
            mm.then_inc(s_modp, UPFRONT)
            ffn(0)
            mlstm()
            ffn(2)
            ffn(3)
            attention()
            ffn(5)
            sums(NLAYERS - 1, 1)
            spread(NLAYERS - 1, 1)
            for b in range(NB):
                pe.wait_ge(s_xnew, xnew_before(NLAYERS) - (KD if b < NB // 2 else 0))
                for d in range(KD):
                    mm = nc.tensor.transpose(psum[:, 2 * b + d // 4, (d % 4) * P:(d % 4 + 1) * P],
                                             xres[:, d, b * P:(b + 1) * P], ident[:, :])
                    if d % 4 == 3:
                        mm.then_inc(s_fT, 1)


GATE_ROW_STEPS = 7 + 3 * NB

_INS = ['x', 'c', 'ada_w', 'ada_b', 'ln_g', 'ln_b', 'ffn_w_in', 'ffn_w_out', 'mlstm_w_in', 'mlstm_gate_bias',
        'mlstm_conv_w', 'mlstm_head_gain', 'mlstm_w_out', 'attn_w_in', 'attn_w_out']


def kernel(**inputs):
    import numpy as _np
    import concourse.bacc as _bacc
    from concourse import mybir as _mybir
    from concourse.bass_utils import run_bass_kernel_spmd as _run

    nc = _bacc.Bacc("TRN2", target_bir_lowering=False, num_devices=1)
    arrays, args = {}, []
    for name in _INS:
        a = _np.ascontiguousarray(inputs[name])
        arrays[f"in_{name}"] = a
        args.append(nc.dram_tensor(f"in_{name}", a.shape, _mybir.dt.from_np(a.dtype), kind="ExternalInput").ap())
    args.append(nc.dram_tensor("out_0", (1, SEQ, D_MODEL), F32, kind="ExternalOutput").ap())
    trunk(nc, *args)
    r = _run(nc, [arrays], core_ids=[0])
    return r.results[0]["out_0"]
```

```python
import math
from contextlib import ExitStack

import concourse.bass as bass
from concourse import mybir

F32 = mybir.dt.float32
F32R = mybir.dt.float32r
ALU = mybir.AluOpType
ACT = mybir.ActivationFunctionType
AX = mybir.AxisListType

P = 128
D_MODEL = 1024
SEQ = 512
D_FF = 2816
DEPTH = 2
N_SUB = 3
NLAYERS = DEPTH * N_SUB
HEADS = 8
DQK = 64
KD = D_MODEL // P
NF = D_FF // P
NB = SEQ // P
ALPHA = (2 * DEPTH) ** 0.25
LN_EPS = 1e-5
RMS_EPS = 1e-6
V_COL = 2 * HEADS * DQK
O_COL = V_COL + D_MODEL
GATE_COL = O_COL + D_MODEL
GROUP_COLS = 3 * D_MODEL
DIL = 4
SCALE = P ** -0.5
MASKED = -1e30

RING = 4
ATT_RING = 3
K_CHUNKS = [(0, 8), (8, 8), (16, 6)]
FFN_UNITS = 2 * NF + len(K_CHUNKS) * KD
MLSTM_UNITS = 4 * KD
HEAD_UNITS = [(0, 0), (0, 1), (1, 0), (1, 1), (2, 0), (2, 1), (0, 2), (1, 2), (2, 2)]
ATT_HEAD_UNITS = len(HEAD_UNITS) * HEADS
FIRST = [0]
for _size in (FFN_UNITS, MLSTM_UNITS, FFN_UNITS, FFN_UNITS, ATT_HEAD_UNITS + KD, FFN_UNITS):
    FIRST.append(FIRST[-1] + _size)
N_UNITS = FIRST[-1]
ATT0, ATT1 = FIRST[4], FIRST[4] + ATT_HEAD_UNITS

CHUNK = 512
CHUNKS = N_SUB * 3 * D_MODEL // CHUNK
ADA_RING = 4
UPFRONT = 4

HALF = SEQ // 2
JOIN = (0, 0, 1, 3)

ATT_BLOCKS = 15
G1_COL, G2_COL = 7 * P, 11 * P

SEG = [0, 512, 896, 1152, 1280]


class Pos:

    def __init__(self, first, step=0, i=None):
        self.first, self.step, self.i = first, step, i

    def __add__(self, n):
        return Pos(self.first + n, self.step, self.i)

    def __sub__(self, n):
        return self + -n

    def __mul__(self, n):
        return Pos(self.first * n, self.step * n, self.i)

    def __floordiv__(self, n):
        assert self.step % n == 0
        return Pos(self.first // n, self.step // n, self.i)

    def __mod__(self, n):
        assert self.step % n == 0
        return self.first % n

    @property
    def at(self):
        return self.i * self.step + self.first if self.step else self.first


def at(first, step, i):
    return Pos(first, step, i) if i is not None else Pos(first)


def pos(x):
    return x if isinstance(x, Pos) else Pos(x)


def wait(eng, sem, count):
    count = pos(count)
    if count.step:
        assert count.first > 0, "a wait in a loop must be for a positive count"
    elif count.first <= 0:
        return
    eng.wait_ge(sem, count.at)


def one(index):
    return bass.ds(pos(index).at, 1)


def slot_of(u):
    u = pos(u)
    return (u - ATT0) % ATT_RING if ATT0 <= u.first < ATT1 else u % RING


def fill_of(u):
    u = pos(u)
    if u.first < ATT0:
        return u // RING + 1
    if u.first < ATT1:
        return (u - ATT0) // ATT_RING + (ATT0 // RING + 1)
    extra = ATT_HEAD_UNITS // ATT_RING if (u - ATT1) % RING < ATT_RING else 0
    return (u - ATT1) // RING + (ATT0 // RING + extra + 1)


def units_before(u):
    u = pos(u)
    if ATT0 + ATT_RING <= u.first < ATT1 + ATT_RING:
        return u - (ATT_RING - 1)
    if u.first == ATT1 + ATT_RING:
        return pos(0)
    return u - (RING - 1)


def trunk(nc, x, c, ada_w, ada_b, ln_g, ln_b, ffn_w_in, ffn_w_out, mlstm_w_in, mlstm_gate_bias,
          mlstm_conv_w, mlstm_head_gain, mlstm_w_out, attn_w_in, attn_w_out, out):
    stack = ExitStack()
    with stack:
        def keep(ctx, name, shape, dt=F32):
            return ctx.enter_context(nc.sbuf_tensor(name, shape, dt))

        def sb(name, shape, dt=F32):
            return keep(stack, name, shape, dt)

        def sem(name):
            return stack.enter_context(nc.semaphore(name))

        xres = sb("xres", [P, KD, SEQ])
        xh = sb("xh", [P, KD, SEQ], F32R)
        xl = sb("xl", [P, KD, SEQ], F32R)
        w_raw = sb("w_raw", [P, RING, KD, P])
        w_hi = sb("w_hi", [P, RING, KD, P], F32R)
        w_lo = sb("w_lo", [P, RING, KD, P], F32R)
        ada_t = sb("ada_t", [P, ADA_RING, CHUNK])
        ada_acc = sb("ada_acc", [P, CHUNK])
        ident = sb("ident", [P, P])
        ones = sb("ones", [P, P])
        cols = sb("cols", [P, 3, P])
        mod = sb("mod", [P, NLAYERS * 3 * KD])
        gate_c = sb("gate_c", [P, NLAYERS * KD])
        mul_c = sb("mul_c", [P, NLAYERS * KD])
        add_c = sb("add_c", [P, NLAYERS * KD])
        cond = sb("cond", [P, KD])
        gbias = sb("gbias", [HEADS, 2])
        eps_c = sb("eps_c", [P, 1])
        ccol = sb("ccol", [P, NB, HEADS])
        mask = sb("mask", [P, 3, P])
        sel4 = sb("sel4", [P, DIL])
        token = sb("token", [1, 8])
        warm = sb("warm", [P, 1])
        sq = sb("sq", [P, SEQ])
        st = sb("st", [P, 2, 5, 2])
        with ExitStack() as r:
            duo = keep(r, "duo", [P, 2, SEQ])
        acc = sb("acc", [P, 2, SEQ])
        with ExitStack() as r:
            xtok = keep(r, "xtok", [P, NB, D_MODEL])
            rows_t = keep(r, "rows_t", [P, 3, P])
            ada_first = keep(r, "ada_first", [P, 2, KD, 2 * CHUNK])
        with ExitStack() as r:
            hh = keep(r, "hh", [P, NF, SEQ], F32R)
            hl = keep(r, "hl", [P, NF, SEQ], F32R)
        with ExitStack() as r:
            sig = keep(r, "sig", [P, HEADS, SEQ])
            qk = keep(r, "qk", [P, KD, SEQ])
            vtok = keep(r, "vtok", [P, NB, D_MODEL])
            with ExitStack() as rr:
                g_raw = keep(rr, "g_raw", [P, KD, P])
                g_hi = keep(rr, "g_hi", [P, KD, P], F32R)
                g_lo = keep(rr, "g_lo", [P, KD, P], F32R)
                grow = keep(rr, "grow", [HEADS, 7, SEQ])
                decay = keep(rr, "decay", [HEADS, SEG[NB] + SEQ])
                conv = keep(rr, "conv", [P, 2, SEQ])
            with ExitStack() as rr:
                drow = keep(rr, "drow", [P, 2, SEG[NB] + SEQ])
                dmat = keep(rr, "dmat", [P, 2, SEG[NB]])
                nsq = keep(rr, "nsq", [P, SEQ])
                den = keep(rr, "den", [P, 2, SEQ])
                yv = keep(rr, "yv", [P, 2, SEQ])
        with ExitStack() as r:
            qT = keep(r, "qT", [P, 3, SEQ])
            kT = keep(r, "kT", [P, 3, SEQ])
            prob = keep(r, "prob", [P, ATT_BLOCKS, P])
            probT = keep(r, "probT", [P, ATT_BLOCKS, P])
            vt = keep(r, "vt", [P, 3, NB, P])
            yh = keep(r, "yh", [P, HEADS, SEQ], F32R)
            yl = keep(r, "yl", [P, HEADS, SEQ], F32R)
            yn = keep(r, "yn", [P, SEQ])
            mx = keep(r, "mx", [P, 3, NB])
            nb = keep(r, "nb", [P, 3, NB])
            dn = keep(r, "dn", [P, 3, NB])
            pm = keep(r, "pm", [P, 2, NB])
            pe12 = keep(r, "pe12", [P, 2, NB])
            pd = keep(r, "pd", [P, 2, NB])
            nm = keep(r, "nm", [P, 2, NB])
            ne = keep(r, "ne", [P, 2, NB])
            nd = keep(r, "nd", [P, 2, NB])
            nj = keep(r, "nj", [P, 2, NB])
            f12 = keep(r, "f12", [P, NB])
            pf = keep(r, "pf", [P, NB])
            fac = keep(r, "fac", [P, 3, NB])
        ln_t = acc[:, :, 0:HALF]
        ln_m = ada_acc[:, :].rearrange("p (j q) -> p j q", q=HALF)
        psum = stack.enter_context(nc.psum_tensor("psum", [P, 8, SEQ], F32))

        def y_of(h):
            return yv[:, h, :] if h < 2 else qk[:, h // 2 - 1 + (HEADS // 2) * (h % 2), :]

        decay_d = nc.dram_tensor("decay_d", [HEADS, SEG[NB] + SEQ], F32, kind="Internal").ap()
        joint_d = nc.dram_tensor("joint_d", [2, SEQ], F32, kind="Internal").ap()
        share_d = nc.dram_tensor("share_d", [SEQ], F32, kind="Internal").ap()

        s_rows = [sem("first_rows_in"), sem("more_rows_in")]
        s_xtok, s_gb = sem("xtok_in"), sem("gate_bias_in")
        s_const, s_mask = sem("consts_made"), sem("mask_steps")
        s_colsT, s_cols, s_cond = sem("cols_transposed"), sem("cols_made"), sem("cond_made")
        s_xT = sem("x_transposed")
        s_raw = [sem(f"unit_in_slot{i}") for i in range(RING)]
        s_hi, s_lo, s_unit = sem("unit_high_made"), sem("unit_low_made"), sem("units_multiplied")
        s_first = [[sem(f"ada_first_in{a}_{k}") for k in range(KD)] for a in range(2)]
        s_ada_in = [sem(f"ada_in_slot{i}") for i in range(ADA_RING)]
        s_ada, s_modp, s_mod, s_der = sem("ada_macs"), sem("mod_summed"), sem("mod_made"), sem("derived")
        s_xnew, s_xhi, s_xm, s_x = sem("xres_tiles"), sem("x_high"), sem("x_modulated"), sem("x_ready")
        s_sg, s_gu, s_hh, s_hl = sem("silu_gate"), sem("hidden"), sem("hidden_high"), sem("hidden_ready")
        s_z, s_sq, s_acc1, s_acc2 = sem("z_tiles"), sem("z_squares"), sem("z_sums"), sem("zz_sums")
        s_tail = sem("first_half_tiles")
        s_stat, s_mom, s_sd, s_rstd, s_bc = (sem("ln_sums"), sem("ln_moment_steps"), sem("ln_sd"),
                                             sem("ln_rstd"), sem("ln_rows_spread"))
        s_warm = sem("table_loads")
        s_row, s_w = sem("ln_row_copied"), sem("ln_scaled")
        s_t, s_tn = sem("ln_centred"), sem("ln_normalised")
        s_ev = sem("projections_out")
        s_gin, s_gz, s_ghi, s_glo, s_gp = (sem("gate_w_in"), sem("gate_w_cleared"), sem("gate_w_high"),
                                           sem("gate_w_low"), sem("gates_multiplied"))
        s_gr, s_ga, s_row_st = sem("gate_row_steps"), sem("gate_row_act_steps"), sem("decay_stored")
        s_og, s_cx, s_qk = sem("output_gate_ready"), sem("conv_steps"), sem("qk_ready")
        s_cf = sem("conv_done")
        s_vt, s_vc = sem("v_transposed"), sem("v_ready")
        s_cT, s_cc = sem("ccol_transposed"), sem("ccol_ready")
        s_rb, s_rbc, s_dm = sem("decay_row_in"), sem("decay_masked"), sem("decay_matrix")
        s_S, s_SD, s_nd = sem("mlstm_scores"), sem("weighted_scores"), sem("num_den")
        s_ab = sem("den_abs")
        s_nsq, s_ms, s_dd, s_dsq, s_tt, s_sdm, s_rr, s_y1, s_y2, s_yh = (
            sem("num_squared"), sem("num_square_mean"), sem("den_bounded"), sem("den_squared"),
            sem("rms_sum"), sem("rms_root"), sem("rms_inverse"), sem("y_normed"), sem("y_gated"),
            sem("y_high"))
        s_yr = sem("y_ready")
        s_as, s_am, s_mxr, s_nb, s_ae = (sem("att_scores"), sem("att_masked"), sem("att_max"),
                                         sem("att_negmax"), sem("att_exp"))
        s_pc, s_pe, s_pst, s_pld, s_nc, s_ne, s_nst, s_nld, s_fac, s_sc = (
            sem("class_stats"), sem("class_exps"), sem("joint_stored"), sem("joint_in"),
            sem("token_stats"), sem("token_exps"), sem("share_stored"), sem("share_in"),
            sem("factor_steps"), sem("prob_scaled"))
        s_pt, s_pta, s_ptd = sem("prob_transposed"), sem("probT_by_act"), sem("probT_by_dve")
        s_o, s_on, s_oe = sem("att_out"), sem("att_out_copied"), sem("att_out_joined")
        s_fT, s_fo, s_fo2, s_out = (sem("out_transposed"), sem("out_by_act"), sem("out_by_dve"),
                                    sem("out_stored"))

        ffn_index = {0: 0, 2: 1, 3: 2, 5: 3}
        START = 2
        EV_START = 4

        def ev_before(n):
            return EV_START + (0 if n == 1 else 3 * KD)

        def ada_chunks(n):
            return {0: UPFRONT, 1: CHUNKS, 2: CHUNKS, 3: CHUNKS + NF // 2}.get(n, 2 * CHUNKS)

        def ada_rounds(n):
            return {0: NF // 2, 2: NF // 2, 3: CHUNKS - NF // 2}.get(n, 0)

        def der_before(n):
            return 4 + 4 * n

        def tail(n):
            return 1 if n in ffn_index else 2

        def d0(n):
            return KD - tail(n)

        def z_before(n):
            return START + sum(d0(k) + 2 * tail(k) for k in range(n))

        def sq_before(n):
            return z_before(n) - START

        def acc_before(n):
            return sum(1 + d0(k) + 2 * (tail(k) - 1) for k in range(n))

        def xnew_before(n):
            return KD + 2 * KD * n

        def tail_before(n):
            return sum(tail(k) for k in range(n))

        def tail_bank(n, half, i):
            return 5 - half if n in ffn_index else 4 + i

        def cols_of(half):
            return slice(half * HALF, (half + 1) * HALF)

        def tail_units(n):
            return 3 if n in ffn_index else 2

        def lead_limit(n):
            return ATT0 + ATT_RING if n == 3 else min(FIRST[n + 1] + RING, N_UNITS)

        w_in_v = [[ffn_w_in[l, j].rearrange("(k p) c -> p k c", p=P) for j in range(2)] for l in range(2)]
        w_out_v = [[ffn_w_out[l, j].rearrange("(k p) c -> p k c", p=P) for j in range(2)] for l in range(2)]
        ml_in_v = mlstm_w_in[0].rearrange("(k p) c -> p k c", p=P)
        ml_out_v = mlstm_w_out[0].rearrange("(k p) c -> p k c", p=P)
        at_in_v = attn_w_in[0].rearrange("(k p) c -> p k c", p=P)
        at_out_v = attn_w_out[0].rearrange("(k p) c -> p k c", p=P)

        def unit_source(u):
            u = pos(u)
            n = max(k for k in range(NLAYERS) if FIRST[k] <= u.first)
            m = u - FIRST[n]
            if n in ffn_index:
                l, j = n // N_SUB, (n % N_SUB) // 2
                if m.first < 2 * NF:
                    col = (m // 2) * P + (m % 2) * D_FF
                    return w_in_v[l][j][:, :, bass.ds(col.at, P)]
                m = m - 2 * NF
                k0, kt = K_CHUNKS[m % 3]
                return w_out_v[l][j][:, k0:k0 + kt, bass.ds(((m // 3) * P).at, P)]
            if n == 1:
                part = m.first // KD
                col = (m - part * KD) * P + (0, V_COL, O_COL, 0)[part]
                return (ml_in_v, ml_in_v, ml_in_v, ml_out_v)[part][:, :, bass.ds(col.at, P)]
            if m.first >= ATT_HEAD_UNITS:
                return at_out_v[:, :, bass.ds(((m - ATT_HEAD_UNITS) * P).at, P)]
            g, which = HEAD_UNITS[m % 9]
            col = (m // 9) * P + g * GROUP_COLS + which * D_MODEL
            return at_in_v[:, :, bass.ds(col.at, P)]

        def ada_share(c0, d):
            if d == 0:
                return c0 + NF // 2, range(KD)
            return c0 + NF // 2 + 1 + (d - 1) // 3, (range(0, 3), range(3, 6), range(6, 8))[(d - 1) % 3]

        FIRST_TILES = [(h, d) for d in range(KD) for h in range(2)]

        block = stack.enter_context(nc.Block())

        @block.sync
        def _(sp):
            def load_unit(u):
                wait(sp, s_lo, units_before(u))
                src = unit_source(u)
                sp.dma_start(w_raw[:, slot_of(u), 0:src.shape[1], :], src).then_inc(s_raw[slot_of(u)], 16)

            def load_ada(ch, ks=range(KD)):
                ch = pos(ch)
                l = ch.first // CHUNKS
                for k in ks:
                    if ch.step or ch.first > UPFRONT or k >= ADA_RING:
                        wait(sp, s_ada, ch * KD + (k - ADA_RING + 1))
                    src = ada_w[l, k * P:(k + 1) * P, bass.ds(((ch - l * CHUNKS) * CHUNK).at, CHUNK)]
                    sp.dma_start(ada_t[:, k % ADA_RING, :], src).then_inc(s_ada_in[k % ADA_RING], 16)

            def load_first(a, k):
                src = ada_w[0, k * P:(k + 1) * P, 0:UPFRONT * CHUNK].rearrange("p (s a q) -> p s a q", s=2, a=2)
                sp.dma_start(ada_first[:, a, k, :].rearrange("p (s q) -> p s q", s=2), src[:, :, a, :]
                             ).then_inc(s_first[a][k], 16)

            def rows(dst, src):
                sp.dma_start(dst, src).then_inc(s_rows[0], 16)

            rows(rows_t[0:48, 0, :], ln_g.rearrange("l s (t q) -> (l s t) q", q=P))
            rows(rows_t[48:96, 0, :], ln_b.rearrange("l s (t q) -> (l s t) q", q=P))
            rows(rows_t[96:104, 0, :], c.rearrange("b (t q) -> (b t) q", q=P))
            rows(rows_t[104:112, 0, :], mlstm_head_gain.rearrange("b (t q) -> (b t) q", q=P))
            for k in range(4):
                load_first(0, k)
            sp.dma_start(xtok[:, :, :], x[0].rearrange("(b p) d -> p b d", p=P)).then_inc(s_xtok, 16)
            for k in range(4, KD):
                load_first(0, k)
            for u in range(RING):
                load_unit(u)
            for k in range(KD):
                load_first(1, k)

            def ffn(n):
                u0, c0 = FIRST[n], ada_chunks(n)

                def in_round(i, start, step, with_ada):
                    for j in range(4):
                        load_unit(Pos(u0 + 4 + j + start, step, i))
                    if with_ada:
                        load_ada(Pos(c0 + start // 4, step // 4, i))

                last = NF // 2 - 1
                r = min(ada_rounds(n) or last, last)
                with sp.Fori(0, r) as i:
                    in_round(i, 0, 4, ada_rounds(n) > 0)
                if r < last:
                    with sp.Fori(0, last - r) as i:
                        in_round(i, 4 * r, 4, False)
                in_round(None, 4 * last, 0, ada_rounds(n) > last)
                o0 = u0 + 2 * NF
                for d in range(KD):
                    for q in range(3):
                        if o0 + 3 * d + 4 + q < lead_limit(n):
                            load_unit(o0 + 3 * d + 4 + q)
                    if n == 0 and d < d0(n):
                        load_ada(*ada_share(c0, d))

            def mlstm():
                u0 = FIRST[1]
                for m in range(MLSTM_UNITS):
                    load_unit(u0 + 4 + m)

            def attention():
                def head(t):
                    for j in range(9):
                        load_unit(t * 9 + (ATT0 + ATT_RING + j))
                with sp.Fori(0, HEADS - 1) as i:
                    head(Pos(0, 1, i))
                head(Pos(HEADS - 1))
                for d in range(-1, KD):
                    load_unit(ATT1 + d + 4)

            ffn(0)
            mlstm()
            ffn(2)
            ffn(3)
            attention()
            ffn(5)
            for b in range(NB):
                sp.wait_ge(s_fo, b + 1)
                sp.wait_ge(s_fo2, b + 1)
                sp.dma_start(out[0, b * P:(b + 1) * P, :], xtok[:, b, :]).then_inc(s_out, 16)
            sp.wait_ge(s_out, 16 * NB)

        @block.gpsimd
        def _(pool):
            for w in range(2):
                nc.gpsimd.dma_start(gbias[:, w:w + 1], mlstm_gate_bias[0, w * HEADS:(w + 1) * HEADS].unsqueeze(1)
                                    ).then_inc(s_gb, 16)
            nc.gpsimd.memset(ident[:, :], 0.0).then_inc(s_const, 1)
            nc.gpsimd.memset(ones[:, :], 1.0).then_inc(s_const, 1)
            nc.gpsimd.memset(eps_c[:, :], LN_EPS / ALPHA ** 2).then_inc(s_const, 1)
            nc.gpsimd.memset(mask[:, :, :], 0.0).then_inc(s_const, 1)
            pool.wait_ge(s_const, 4)
            nc.gpsimd.affine_select(out=ident[:, :], in_=ident[:, :], compare_op=ALU.not_equal, fill=1.0,
                                    base=0, pattern=[[-1, P]], channel_multiplier=1).then_inc(s_const, 1)
            nc.gpsimd.affine_select(out=mask[:, 0, :], in_=mask[:, 0, :], compare_op=ALU.is_ge, fill=MASKED,
                                    base=0, pattern=[[1, P]], channel_multiplier=-1).then_inc(s_const, 1)
            nc.gpsimd.affine_select(out=mask[:, 1, :], in_=mask[:, 1, :], compare_op=ALU.is_ge, fill=MASKED,
                                    base=0, pattern=[[-1, P]], channel_multiplier=1).then_inc(s_const, 1)

            def z_sums(n, tiles):
                for d, half, k in tiles:
                    c = slice(0, SEQ) if half is None else cols_of(half)
                    a = k - (half or 0)
                    pool.wait_ge(s_z, z_before(n) + k + 1)
                    pool.wait_ge(s_acc1, acc_before(n) + a + 1)
                    nc.gpsimd.tensor_tensor(acc[:, 0, c], acc[:, 0, c], xres[:, d, c], ALU.add).then_inc(s_acc1, 1)
                    pool.wait_ge(s_sq, sq_before(n) + k + 1)
                    pool.wait_ge(s_acc2, acc_before(n) + a + 1)
                    nc.gpsimd.tensor_tensor(acc[:, 1, c], acc[:, 1, c], sq[:, c], ALU.add).then_inc(s_acc2, 1)

            def scale(n, half, ds):
                if n + 1 == NLAYERS:
                    return
                for d in ds:
                    pool.wait_ge(s_row, 2 * n + half + 1)
                    pool.wait_ge(s_t, 2 * KD * n + KD * half + d + 1)
                    nc.gpsimd.tensor_tensor(xres[:, d, cols_of(half)], ln_t[:, d % 2, :], sq[:, cols_of(half)],
                                            ALU.mult).then_inc(s_w, 1)

            def sublayer_end(n):
                z_sums(n, [(d, None, d) for d in range(d0(n))])
                z_sums(n, [(d0(n) + i, 0, d0(n) + i) for i in range(tail(n) - 1)])
                scale(n, 0, (0, 1))
                z_sums(n, [(d0(n) + i, 1, d0(n) + tail(n) + i) for i in range(tail(n) - 1)])
                scale(n, 0, range(2, KD))
                scale(n, 1, range(KD))

            sublayer_end(0)
            pool.wait_ge(s_unit, FIRST[1])
            nc.gpsimd.memset(g_raw[:, :, :], 0.0).then_inc(s_gz, 1)
            pool.wait_ge(s_gz, 1)
            for w in range(2):
                nc.gpsimd.dma_start(g_raw[:, :, 32 * w:32 * w + HEADS],
                                    ml_in_v[:, :, GATE_COL + w * HEADS:GATE_COL + (w + 1) * HEADS]
                                    ).then_inc(s_gin, 16)
            pool.wait_ge(s_gr, GATE_ROW_STEPS)
            pool.wait_ge(s_ga, 4)
            nc.gpsimd.dma_start(decay_d, decay[:, :]).then_inc(s_row_st, 16)
            pool.wait_ge(s_row_st, 16)
            pool.wait_ge(s_cT, 1)
            pool.wait_ge(s_qk, START + KD)
            pool.wait_ge(s_gp, 1)
            for h in range(HEADS):
                if h >= 2:
                    pool.wait_ge(s_dd, h - 1)
                    pool.wait_ge(s_dm, 4 * (h - 1))
                nc.gpsimd.dma_start(drow[:, h % 2, :], decay_d[h].partition_broadcast(P)).then_inc(s_rb, 16)
                pool.wait_ge(s_rb, 16 * (h + 1))
                for j in range(NB):
                    seg = drow[:, h % 2, SEG[j]:SEG[j] + P]
                    nc.gpsimd.affine_select(out=seg, in_=seg, compare_op=ALU.is_ge, fill=MASKED, base=0,
                                            pattern=[[1, P]], channel_multiplier=-1).then_inc(s_rbc, 1)

            sublayer_end(1)
            sublayer_end(2)
            sublayer_end(3)

            def exchange(t):
                wait(pool, s_pc, t * 6 + 6)
                nc.gpsimd.dma_start(joint_d.rearrange("a (i r) -> i a r", r=NB), pm[:, :, :]).then_inc(s_pst, 16)
                wait(pool, s_pst, t * 16 + 16)
                nc.gpsimd.dma_start(nm[:, :, :], joint_d.rearrange("a (b p) -> p a b", p=P),
                                    allow_slow_non_contiguous=True).then_inc(s_pld, 16)
                wait(pool, s_nc, t * 8 + 8)
                nc.gpsimd.dma_start(share_d.rearrange("(b p) -> p b", p=P), f12[:, :],
                                    allow_slow_non_contiguous=True).then_inc(s_nst, 16)
                wait(pool, s_nst, t * 16 + 16)
                nc.gpsimd.dma_start(pf[:, :], share_d.rearrange("(i r) -> i r", r=NB)).then_inc(s_nld, 16)

            for t in range(HEADS):
                exchange(Pos(t))
            sublayer_end(4)
            sublayer_end(5)

        @block.scalar
        def _(act):
            def high(u):
                s = slot_of(u)
                wait(act, s_raw[s], fill_of(u) * 16)
                wait(act, s_unit, units_before(u))
                nc.scalar.activation(w_hi[:, s], w_raw[:, s], ACT.Copy).then_inc(s_hi, 1)

            def square(n, d):
                wait(act, s_z, d + (z_before(n) + 1))
                wait(act, s_acc2, d + (acc_before(n) + 1))
                nc.scalar.activation(sq[:, :], xres[:, one(d), :], ACT.Square).then_inc(s_sq, 1)

            def tail_squares(n, half):
                for i in range(tail(n)):
                    act.wait_ge(s_z, z_before(n) + d0(n) + tail(n) * half + i + 1)
                    act.wait_ge(s_acc2, acc_before(n) + 1 + d0(n) + (tail(n) - 1) * half + i)
                    nc.scalar.activation(sq[:, cols_of(half)], xres[:, d0(n) + i, cols_of(half)], ACT.Square
                                         ).then_inc(s_sq, 1)

            def ln_root(n, half):
                act.wait_ge(s_mom, 3 * (2 * n + half + 1))
                nc.scalar.activation(st[:, half, 3, :], st[:, half, 2, :], ACT.Sqrt, bias=eps_c[:, :]
                                     ).then_inc(s_sd, 1)

            def high_x(n, half, d, src, scale=1.0):
                nc.scalar.activation(xh[:, d, cols_of(half)], src, ACT.Identity,
                                     bias=add_c[:, d + n * KD:d + n * KD + 1], scale=scale).then_inc(s_xhi, 1)

            def residual(n, half, d):
                act.wait_ge(s_w, 2 * KD * n + KD * half + d + 1)
                nc.scalar.activation(xres[:, d, cols_of(half)], xres[:, d, cols_of(half)], ACT.Identity,
                                     bias=cols[:, 0, 48 + n * KD + d:49 + n * KD + d],
                                     scale=cols[:, 0, n * KD + d:n * KD + d + 1]).then_inc(s_xnew, 1)

            def ln_tiles(n, half, ds):
                for a in ds[::2]:
                    if n + 1 < NLAYERS:
                        for d in (a, a + 1):
                            act.wait_ge(s_tn, 2 * KD * n + KD * half + d + 1)
                            high_x(n + 1, half, d, ln_m[:, d % 2, :])
                        behind = range(a - 2 if a else 0, a if a + 2 < KD else KD)
                    else:
                        behind = (a, a + 1)
                    for d in behind:
                        residual(n, half, d)

            def layer_norm(n):
                lead = [u for u in range(FIRST[n + 1] + 4 - tail_units(n), FIRST[n + 1] + 4) if u < lead_limit(n)]
                tail_squares(n, 0)
                if tail_units(n) == 3 and lead:
                    high(lead.pop(0))
                ln_root(n, 0)
                if lead:
                    high(lead.pop(0))
                ln_tiles(n, 0, (0, 1))
                tail_squares(n, 1)
                if lead:
                    high(lead.pop(0))
                ln_tiles(n, 0, (2, 3))
                ln_root(n, 1)
                if n in (0, 1, 2, 4):
                    nc.scalar.activation(warm[:, :], eps_c[:, :], ACT.Silu).then_inc(s_warm, 1)
                ln_tiles(n, 0, range(4, KD))
                ln_tiles(n, 1, range(KD))

            def ffn(n):
                u0, h0 = FIRST[n], NF * ffn_index[n]
                act.wait_ge(s_xnew, xnew_before(n))

                with act.Fori(0, NF // 2) as i:
                    for j in range(2):
                        f = Pos(j, 2, i)
                        u = Pos(u0 + 2 * j, 4, i)
                        wait(act, s_unit, u + 1)
                        wait(act, s_hl, f + (START + h0 - 1))
                        nc.scalar.activation(duo[:, j, :], psum[:, 2 * j, :], ACT.Silu).then_inc(s_sg, 1)
                        high(u + 4)
                        wait(act, s_gu, f + (START + h0 + 1))
                        nc.scalar.activation(hh[:, one(f), :], duo[:, j:j + 1, :], ACT.Copy).then_inc(s_hh, 1)
                        high(u + 5)

                for d in range(d0(n)):
                    u = u0 + 2 * NF + 3 * d
                    high(u + 4)
                    high(u + 5)
                    square(n, d)
                    if u + 6 < lead_limit(n):
                        high(u + 6)
                layer_norm(n)

            def gates():
                act.wait_ge(s_gr, 3)
                nc.scalar.activation(grow[:, 2, :], grow[:, 1, :], ACT.Abs).then_inc(s_ga, 1)
                act.wait_ge(s_ga, 1)
                nc.scalar.activation(grow[:, 2, :], grow[:, 2, :], ACT.Exp, scale=-1.0).then_inc(s_ga, 1)
                act.wait_ge(s_ga, 2)
                nc.scalar.activation(grow[:, 2, :], grow[:, 2, :], ACT.Ln, bias=ones[0:HEADS, 0:1]).then_inc(s_ga, 1)

            def gate_floor():
                act.wait_ge(s_gr, 7)
                nc.scalar.activation(decay[:, SEG[NB]:], grow[:, 5, :], ACT.Exp, scale=-1.0).then_inc(s_ga, 1)

            def mlstm():
                n, u0, e0 = 1, FIRST[1], ev_before(1)
                act.wait_ge(s_xnew, xnew_before(n))
                def raw_out(m):
                    act.wait_ge(s_unit, u0 + m + 1)
                    act.wait_ge(s_cf, m + START - 1)
                    nc.scalar.activation(duo[:, m % 2, :], psum[:, m % 4, :], ACT.Copy).then_inc(s_ev, 1)
                    high(u0 + m + 4)

                raw_out(0)
                for m in range(KD):
                    if m + 1 < KD:
                        raw_out(m + 1)
                    act.wait_ge(s_cf, m + START + 1)
                    nc.scalar.activation(qk[:, m, :], conv[:, m % 2, :], ACT.Silu).then_inc(s_qk, 1)
                    if m == 1:
                        act.wait_ge(s_gin, 32)
                        nc.scalar.activation(g_hi[:, :, :], g_raw[:, :, :], ACT.Copy).then_inc(s_ghi, 1)
                    if m == 3:
                        gates()
                    if m == 5:
                        gate_floor()
                with act.Fori(0, 2) as i:
                    for j in range(4):
                        m = Pos(KD + j, 4, i)
                        wait(act, s_unit, m + (u0 + 1))
                        wait(act, s_vt, m - KD + (START - 1))
                        nc.scalar.activation(duo[:, j % 2, :], psum[:, j, :], ACT.Copy).then_inc(s_ev, 1)
                        high(m + (u0 + 4))

                def gate_out(h):
                    act.wait_ge(s_unit, u0 + 2 * KD + h + 1)
                    nc.scalar.activation(sig[:, h, :], psum[:, 6, :], ACT.Copy).then_inc(s_ev, 1)
                    high(u0 + 2 * KD + h + 4)

                def decay_matrix(h):
                    if h >= 2:
                        act.wait_ge(s_nd, h - 1)
                    act.wait_ge(s_rbc, 4 * (h + 1))
                    for b in range(NB):
                        nc.scalar.activation(dmat[:, h % 2, SEG[b]:SEG[b + 1]], drow[:, h % 2, SEG[b]:SEG[b + 1]],
                                             ACT.Exp, bias=ccol[:, b, h:h + 1]).then_inc(s_dm, 1)

                gate_out(0)
                act.wait_ge(s_cc, 1)
                decay_matrix(0)
                gate_out(1)
                for h in range(HEADS):
                    if h + 1 < HEADS:
                        decay_matrix(h + 1)
                    act.wait_ge(s_nd, h + 1)
                    if h >= 1:
                        act.wait_ge(s_ms, h)
                    nc.scalar.activation(nsq[:, :], psum[:, 3 + h % 2, :], ACT.Square).then_inc(s_nsq, 1)
                    if h >= 2:
                        act.wait_ge(s_y1, h - 1)
                    nc.scalar.activation(den[:, h % 2, :], psum[:, 5, :], ACT.Abs).then_inc(s_ab, 1)
                    act.wait_ge(s_dd, h + 1)
                    nc.scalar.activation(den[:, h % 2, :], den[:, h % 2, :], ACT.Square,
                                         scale=math.sqrt(RMS_EPS)).then_inc(s_dsq, 1)
                    if h + 2 < HEADS - 1:
                        gate_out(h + 2)
                    act.wait_ge(s_tt, h + 1)
                    nc.scalar.activation(den[:, h % 2, :], den[:, h % 2, :], ACT.Sqrt).then_inc(s_sdm, 1)

                def sigmoid(h):
                    nc.scalar.activation(sig[:, h, :], sig[:, h, :], ACT.Sigmoid).then_inc(s_og, 1)

                act.wait_ge(s_ev, e0 + 3 * KD - 1)
                for h in range(3):
                    sigmoid(h)
                gate_out(HEADS - 1)
                act.wait_ge(s_ev, e0 + 3 * KD)
                for h in range(HEADS):
                    act.wait_ge(s_y2, h + 1)
                    nc.scalar.activation(xh[:, h, :], y_of(h), ACT.Copy).then_inc(s_yh, 1)
                    if h + 3 < HEADS:
                        sigmoid(h + 3)

                for d in range(d0(n)):
                    high(u0 + 3 * KD + 4 + d)
                    square(n, d)
                layer_norm(n)

            def attention():
                n, e0 = 4, ev_before(4)
                act.wait_ge(s_xnew, xnew_before(n))

                def head(t, prev):
                    for j in range(9):
                        m = t * 9 + j
                        g, which = HEAD_UNITS[j]
                        wait(act, s_unit, m + (ATT0 + 1))
                        src = psum[:, j % 3, :]
                        if g:
                            src = src.rearrange("p (i r) -> p r i", r=DIL)
                        if which < 2:
                            if which == 0 and g == 0:
                                wait(act, s_as, t)
                            dst = (qT, kT)[which][:, g, :]
                        else:
                            wait(act, s_vt, t * 3 + (START + KD + g - 1))
                            dst = duo[:, g % 2, :]
                        if g:
                            dst = dst.rearrange("p (r i) -> p r i", r=DIL)
                        high(m + (ATT0 + ATT_RING))
                        nc.scalar.activation(dst, src, ACT.Copy).then_inc(s_ev, 1)
                        if prev is not None:
                            if j == 1:
                                token_exps(prev)
                            if j == 4:
                                prob_out(prev)
                            if j == 5:
                                out_copy(prev)
                            if j == 6:
                                out_high(prev)
                        if j == 7:
                            exps(t)
                        if j == 8:
                            class_exps(t)

                def exps(t):
                    wait(act, s_nb, t + 1)
                    for g in range(3):
                        for b in range(NB):
                            if g == 0:
                                lo, n_b = (0, 1) if b == 0 else (2 * b - 1, 2)
                            else:
                                lo, n_b = (7, 11)[g - 1] + b, 1
                            blk = prob[:, lo:lo + n_b, :]
                            nc.scalar.activation(blk, blk, ACT.Exp, bias=nb[:, g, b:b + 1], scale=SCALE,
                                                 accum_out=dn[:, g, b:b + 1]).then_inc(s_ae, 1)

                def class_exps(t):
                    wait(act, s_pc, t * 6 + 3)
                    nc.scalar.activation(pe12[:, :, :], pd[:, :, :], ACT.Exp, scale=SCALE).then_inc(s_pe, 1)

                def token_exps(t):
                    wait(act, s_nc, t * 8 + 3)
                    nc.scalar.activation(ne[:, :, :], nj[:, :, :], ACT.Exp, scale=SCALE).then_inc(s_ne, 1)

                def prob_out(t):
                    wait(act, s_pt, t + 1)
                    for bank in (3, 5):
                        b0 = (bank - 3) * 4
                        nc.scalar.activation(probT[:, b0:b0 + 4, :].rearrange("p b q -> p (b q)"),
                                             psum[:, bank, :], ACT.Copy).then_inc(s_pta, 1)

                def out_copy(t):
                    wait(act, s_o, t + 1)
                    nc.scalar.activation(yn[:, :], psum[:, 7, :], ACT.Copy).then_inc(s_on, 1)

                def out_high(t):
                    wait(act, s_oe, t + 1)
                    nc.scalar.activation(yh[:, one(t), :], yn[:, :].unsqueeze(1), ACT.Copy).then_inc(s_yh, 1)

                head(Pos(0), None)
                with act.Fori(0, HEADS - 1) as i:
                    head(Pos(1, 1, i), Pos(0, 1, i))
                t = Pos(HEADS - 1)
                high(ATT1 + ATT_RING)
                token_exps(t)
                prob_out(t)
                out_copy(t)
                out_high(t)
                for d in range(d0(n)):
                    high(ATT1 + 4 + d)
                    square(n, d)
                layer_norm(n)

            def rows(dst, src):
                act.dma_start(dst, src).then_inc(s_rows[1], 16)

            rows(rows_t[0:72, 1, :], ada_b[0].rearrange("(t q) -> t q", q=P))
            rows(rows_t[72:104, 1, :], mlstm_conv_w[0].rearrange("j (t q) -> (j t) q", q=P))
            rows(rows_t[0:72, 2, :], ada_b[1].rearrange("(t q) -> t q", q=P))
            act.wait_ge(s_cols, 1)
            nc.scalar.activation(cond[:, :], cols[:, 0, 96:104], ACT.Silu).then_inc(s_cond, 1)
            for d in range(KD):
                act.wait_ge(s_xT, d + 1)
                nc.scalar.activation(xres[:, d, :], psum[:, d % 4, :], ACT.Copy).then_inc(s_xnew, 1)
            for u in range(RING):
                high(u)
            for a, (half, d) in enumerate(FIRST_TILES):
                if a % KD == 0:
                    act.wait_ge(s_der, 2 + 2 * (a // KD))
                act.wait_ge(s_xnew, d + 1)
                high_x(0, half, d, xres[:, d, cols_of(half)], mul_c[:, d:d + 1])
            ffn(0)
            mlstm()
            ffn(2)
            ffn(3)
            attention()
            ffn(5)
            for b in range(NB):
                act.wait_ge(s_fT, 2 * b + 1)
                nc.scalar.activation(xtok[:, b, 0:SEQ], psum[:, 2 * b, :], ACT.Copy).then_inc(s_fo, 1)

        @block.vector
        def _(dve):
            def low(u):
                s = slot_of(u)
                wait(dve, s_hi, pos(u) + 1)
                nc.vector.tensor_tensor(w_lo[:, s], w_raw[:, s], w_hi[:, s].bitcast(F32),
                                        ALU.subtract).then_inc(s_lo, 1)

            def ada(ch, ks=range(KD)):
                ch = pos(ch)
                for k in ks:
                    s = k % ADA_RING
                    wait(dve, s_ada_in[s], (ch - UPFRONT) * 32 + 16 * (k // ADA_RING + 1))
                    if k == 0:
                        wait(dve, s_modp, ch)
                        nc.vector.tensor_scalar(ada_acc[:, :], ada_t[:, s, :], cond[:, 0:1], None,
                                                ALU.mult).then_inc(s_ada, 1)
                    else:
                        wait(dve, s_ada, ch * KD + k)
                        nc.vector.scalar_tensor_tensor(out=ada_acc[:, :], in0=ada_t[:, s, :],
                                                       scalar=cond[:, k:k + 1], in1=ada_acc[:, :],
                                                       op0=ALU.mult, op1=ALU.add).then_inc(s_ada, 1)

            def mod_column(ch):
                ch = pos(ch)
                l = ch.first // CHUNKS
                wait(dve, s_modp, ch + 1)
                nc.vector.tensor_tensor(mod[:, bass.ds((ch * 4).at, 4)], psum[:, 7, 0:4],
                                        cols[:, 1 + l, bass.ds(((ch - l * CHUNKS) * 4).at, 4)],
                                        ALU.add).then_inc(s_mod, 1)

            def derive(n, weight):
                c0, d0 = 3 * KD * n, der_before(n)
                wait(dve, s_mod, min((c0 + 5 * KD) // 4, 2 * CHUNKS))
                nc.vector.tensor_scalar(gate_c[:, n * KD:(n + 1) * KD], mod[:, c0 + 2 * KD:c0 + 3 * KD], 1.0,
                                        weight / ALPHA, ALU.add, ALU.mult).then_inc(s_der, 1)
                if n + 1 == NLAYERS:
                    return
                c1, k1 = c0 + 3 * KD, (n + 1) * KD
                nc.vector.scalar_tensor_tensor(out=mul_c[:, k1:k1 + KD], in0=mod[:, c1 + KD:c1 + 2 * KD],
                                               scalar=1.0, in1=cols[:, 0, n * KD:(n + 1) * KD],
                                               op0=ALU.add, op1=ALU.mult).then_inc(s_der, 1)
                nc.vector.scalar_tensor_tensor(out=add_c[:, k1:k1 + KD], in0=mod[:, c1 + KD:c1 + 2 * KD],
                                               scalar=1.0, in1=cols[:, 0, 48 + n * KD:48 + (n + 1) * KD],
                                               op0=ALU.add, op1=ALU.mult).then_inc(s_der, 1)
                dve.wait_ge(s_der, d0 + 3)
                nc.vector.tensor_tensor(add_c[:, k1:k1 + KD], add_c[:, k1:k1 + KD], mod[:, c1:c1 + KD],
                                        ALU.add).then_inc(s_der, 1)

            def clear_sums(n):
                dve.wait_ge(s_der, der_before(n) + 1)
                nc.vector.memset(acc[:, 0, :], 0.0).then_inc(s_acc1, 1)
                nc.vector.memset(acc[:, 1, :], 0.0).then_inc(s_acc2, 1)

            def z_tile(n, d, bank, unit):
                dve.wait_ge(s_unit, unit + 1)
                dve.wait_ge(s_xnew, xnew_before(n))
                nc.vector.scalar_tensor_tensor(out=xres[:, d, :], in0=psum[:, bank, :],
                                               scalar=gate_c[:, n * KD + d:n * KD + d + 1], in1=xres[:, d, :],
                                               op0=ALU.mult, op1=ALU.add).then_inc(s_z, 1)

            def z_tail(n, half, unit):
                c = cols_of(half)
                for i in range(tail(n)):
                    d = d0(n) + i
                    if half == 0:
                        dve.wait_ge(s_tail, tail_before(n) + i + 1)
                    else:
                        dve.wait_ge(s_unit, unit + i + 1)
                    nc.vector.scalar_tensor_tensor(out=xres[:, d, c], in0=psum[:, tail_bank(n, half, i), c],
                                                   scalar=gate_c[:, n * KD + d:n * KD + d + 1], in1=xres[:, d, c],
                                                   op0=ALU.mult, op1=ALU.add).then_inc(s_z, 1)

            def ln_moments(n, half):
                k = 3 * (2 * n + half)
                dve.wait_ge(s_stat, 2 * n + half + 1)
                nc.vector.tensor_scalar(st[:, half, 0, :], psum[:, 6 + half, 0:2], -1 / D_MODEL, None, ALU.mult
                                        ).then_inc(s_mom, 1)
                dve.wait_ge(s_mom, k + 1)
                nc.vector.tensor_tensor(st[:, half, 1, :], st[:, half, 0, :], st[:, half, 0, :], ALU.mult
                                        ).then_inc(s_mom, 1)
                dve.wait_ge(s_mom, k + 2)
                nc.vector.scalar_tensor_tensor(out=st[:, half, 2, :], in0=psum[:, 6 + half, 2:4], scalar=1 / D_MODEL,
                                               in1=st[:, half, 1, :], op0=ALU.mult, op1=ALU.subtract
                                               ).then_inc(s_mom, 1)

            def ln_inverse(n, half):
                dve.wait_ge(s_sd, 2 * n + half + 1)
                nc.vector.reciprocal(st[:, half, 4, :], st[:, half, 3, :]).then_inc(s_rstd, 1)

            def ln_tiles(n, half, ds):
                k = 2 * KD * n + KD * half
                def centre(d):
                    if k + d > 1:
                        dve.wait_ge(s_w, k + d - 1)
                    dve.wait_ge(s_bc, 2 * n + half + 1)
                    nc.vector.tensor_tensor(ln_t[:, d % 2, :], psum[:, 6 + half, 0:HALF], xres[:, d, cols_of(half)],
                                            ALU.add).then_inc(s_t, 1)

                def normalise(d):
                    dve.wait_ge(s_t, k + d + 1)
                    if n + 1 < NLAYERS:
                        dve.wait_ge(s_x, 2 * KD + k + d - 1)
                        dst, factor = ln_m[:, d % 2, :], mul_c[:, (n + 1) * KD + d:(n + 1) * KD + d + 1]
                    else:
                        dst, factor = xres[:, d, cols_of(half)], 1.0
                    nc.vector.scalar_tensor_tensor(out=dst, in0=ln_t[:, d % 2, :], scalar=factor,
                                                   in1=psum[:, 6 + half, HALF:], op0=ALU.mult, op1=ALU.mult
                                                   ).then_inc(s_tn if n + 1 < NLAYERS else s_w, 1)

                for a in ds[::2]:
                    centre(a)
                    if a == 0:
                        normalise(a)
                        centre(a + 1)
                        normalise(a + 1)
                        if n + 1 < NLAYERS:
                            nc.vector.tensor_copy(sq[:, cols_of(half)], psum[:, 6 + half, HALF:]).then_inc(s_row, 1)
                    else:
                        centre(a + 1)
                        normalise(a)
                        normalise(a + 1)
                    if n + 1 < NLAYERS:
                        for d in (a, a + 1):
                            dve.wait_ge(s_tn, k + d + 1)
                            dve.wait_ge(s_xhi, 2 * KD + k + d + 1)
                            nc.vector.scalar_tensor_tensor(out=xl[:, d, cols_of(half)], in0=ln_m[:, d % 2, :],
                                                           scalar=add_c[:, (n + 1) * KD + d:(n + 1) * KD + d + 1],
                                                           in1=xh[:, d, cols_of(half)].bitcast(F32), op0=ALU.add,
                                                           op1=ALU.subtract).then_inc(s_x, 1)

            def layer_norm(n):
                lead = [u for u in range(FIRST[n + 1] + 4 - tail_units(n), FIRST[n + 1] + 4) if u < lead_limit(n)]
                last = FIRST[n + 1] - tail(n)
                z_tail(n, 0, last)
                if n == 0:
                    mod_column(ada_chunks(n) + NF // 2 + 2)
                ln_moments(n, 0)
                if tail_units(n) == 3 and lead:
                    low(lead.pop(0))
                ln_inverse(n, 0)
                ln_tiles(n, 0, (0, 1))
                if lead:
                    low(lead.pop(0))
                z_tail(n, 1, last)
                ln_tiles(n, 0, (2, 3))
                if lead:
                    low(lead.pop(0))
                ln_moments(n, 1)
                ln_inverse(n, 1)
                ln_tiles(n, 0, range(4, KD))
                ln_tiles(n, 1, range(KD))

            def ffn(n):
                u0, h0, c0 = FIRST[n], NF * ffn_index[n], ada_chunks(n)
                dve.wait_ge(s_x, 2 * (n + 1) * KD)

                def in_round(i, start, with_ada):
                    for j in range(2):
                        f = at(2 * start + j, 2, i)
                        u = at(u0 + 4 * start + 2 * j, 4, i)
                        wait(dve, s_sg, f + (h0 + 1))
                        wait(dve, s_unit, u + 2)
                        nc.vector.tensor_tensor(duo[:, j, :], duo[:, j, :], psum[:, 2 * j + 1, :],
                                                ALU.mult).then_inc(s_gu, 1)
                        low(u + 4)
                        wait(dve, s_hh, f + (h0 + 1))
                        wait(dve, s_gu, f + (START + h0 + 1))
                        nc.vector.tensor_tensor(hl[:, one(f), :], duo[:, j:j + 1, :],
                                                hh[:, one(f), :].bitcast(F32), ALU.subtract).then_inc(s_hl, 1)
                        low(u + 5)
                        if with_ada and j == 0:
                            if start:
                                mod_column(at(c0 + start - 1, 1, i))
                            ada(at(c0 + start, 1, i))

                if ada_rounds(n):
                    in_round(None, 0, True)
                    with dve.Fori(0, ada_rounds(n) - 1) as i:
                        in_round(i, 1, True)
                if ada_rounds(n) < NF // 2:
                    with dve.Fori(0, NF // 2 - ada_rounds(n)) as i:
                        in_round(i, ada_rounds(n), False)
                derive(n, 0.5)
                clear_sums(n)

                for d in range(d0(n)):
                    u = u0 + 2 * NF + 3 * d
                    low(u + 4)
                    low(u + 5)
                    z_tile(n, d, 4 + d % 2, u + 2)
                    if u + 6 < lead_limit(n):
                        low(u + 6)
                    if d == 0 and ada_rounds(n):
                        mod_column(c0 + ada_rounds(n) - 1)
                    if n == 0:
                        if d in (1, 4):
                            mod_column(c0 + NF // 2 + d // 4)
                        ada(*ada_share(c0, d))
                layer_norm(n)

            def step(ins):
                ins.then_inc(s_gr, 1)

            def gate_rows():
                dve.wait_ge(s_gp, 1)
                dve.wait_ge(s_gb, 32)
                step(nc.vector.tensor_scalar(grow[:, 0, :], psum[0:HEADS, 6, :], gbias[:, 0:1], None, ALU.add))
                step(nc.vector.tensor_copy(grow[:, 1, :], psum[32:32 + HEADS, 6, :]))
                dve.wait_ge(s_gr, 2)
                step(nc.vector.tensor_scalar(grow[:, 1, :], grow[:, 1, :], gbias[:, 1:2], None, ALU.add))
                dve.wait_ge(s_gr, 3)
                step(nc.vector.tensor_scalar(grow[:, 3, :], grow[:, 1, :], 0.0, None, ALU.min))
                step(nc.vector.memset(grow[:, 4, :], 0.0))

            def gate_scans():
                dve.wait_ge(s_ga, 3)
                dve.wait_ge(s_gr, 5)
                step(nc.vector.tensor_tensor(grow[:, 3, :], grow[:, 3, :], grow[:, 2, :], ALU.subtract))
                dve.wait_ge(s_gr, 6)
                step(nc.vector.tensor_tensor_scan(grow[:, 5, :], grow[:, 3, :], grow[:, 0, :], 0.0,
                                                  ALU.add, ALU.max))
                for b in range(NB):
                    step(nc.vector.tensor_tensor_scan(decay[:, SEG[b]:SEG[b + 1]], grow[:, 3, b * P:],
                                                      grow[:, 4, b * P:], 0.0, ALU.add, ALU.add))

            def decay_rows():
                dve.wait_ge(s_gr, 7 + NB)
                for b in range(NB):
                    step(nc.vector.tensor_tensor(grow[:, 6, b * P:(b + 1) * P], grow[:, 0, b * P:(b + 1) * P],
                                                 decay[:, SEG[b]:SEG[b] + P], ALU.subtract))
                dve.wait_ge(s_gr, 7 + 2 * NB)
                for b in range(NB):
                    step(nc.vector.tensor_tensor(decay[:, SEG[b]:SEG[b + 1]], decay[:, SEG[b]:SEG[b + 1]],
                                                 grow[:, 5, b * P:], ALU.subtract))

            gate_steps = (gate_rows, gate_scans, decay_rows)

            def mlstm():
                n, u0 = 1, FIRST[1]
                dve.wait_ge(s_x, 2 * (n + 1) * KD)
                for half in range(2):
                    for j in range(4):
                        m, s = 4 * half + j, j % 2
                        low(u0 + m + 4)
                        dve.wait_ge(s_ev, ev_before(1) + m + 1)
                        dve.wait_ge(s_qk, m + START - 1)
                        tap = lambda k: cols[:, 1, 72 + KD * k + m:73 + KD * k + m]
                        nc.vector.tensor_scalar(conv[:, s, :], duo[:, s, :], tap(3), None, ALU.mult).then_inc(s_cx, 1)
                        for k in (1, 2, 3):
                            dve.wait_ge(s_cx, m * 3 + k)
                            nc.vector.scalar_tensor_tensor(out=conv[:, s, k:], in0=duo[:, s, :SEQ - k],
                                                           scalar=tap(3 - k), in1=conv[:, s, k:],
                                                           op0=ALU.mult, op1=ALU.add
                                                           ).then_inc(s_cf if k == 3 else s_cx, 1)
                        if m == 1:
                            dve.wait_ge(s_ghi, 1)
                            nc.vector.tensor_tensor(g_lo[:, :, :], g_raw[:, :, :], g_hi[:, :, :].bitcast(F32),
                                                    ALU.subtract).then_inc(s_glo, 1)
                        if 3 <= m < 6:
                            gate_steps[m - 3]()
                with dve.Fori(0, 2) as i:
                    for j in range(4):
                        m = Pos(j, 4, i)
                        low(m + (u0 + KD + 4))
                        wait(dve, s_vt, m + (START + 1))
                        nc.vector.tensor_copy(vtok[:, :, bass.ds((m * P).at, P)],
                                              psum[:, 4 + j % 2, :].rearrange("p (b q) -> p b q", q=P)
                                              ).then_inc(s_vc, 1)
                dve.wait_ge(s_cT, 1)
                nc.vector.tensor_copy(ccol[:, :, :], psum[:, 7, 0:NB * HEADS].rearrange("p (b h) -> p b h", h=HEADS)
                                      ).then_inc(s_cc, 1)
                derive(n, 1.0)

                def weigh(h):
                    dve.wait_ge(s_S, h + 1)
                    dve.wait_ge(s_dm, 4 * (h + 1))
                    for bank, lo, hi in ((0, SEG[0], SEG[1]), (1, SEG[1], SEG[2]), (2, SEG[2], SEG[4])):
                        nc.vector.scalar_tensor_tensor(out=dmat[:, h % 2, lo:hi], in0=psum[:, bank, 0:hi - lo],
                                                       scalar=DQK ** -0.5, in1=dmat[:, h % 2, lo:hi],
                                                       op0=ALU.mult, op1=ALU.mult).then_inc(s_SD, 1)

                clear_sums(n)
                low(u0 + 2 * KD + 4)
                weigh(0)
                low(u0 + 2 * KD + 5)
                for h in range(HEADS):
                    s = h % 2
                    dve.wait_ge(s_ab, h + 1)
                    nc.vector.tensor_tensor(den[:, s, :], den[:, s, :], drow[:, s, SEG[NB]:], ALU.max
                                            ).then_inc(s_dd, 1)
                    if h + 1 < HEADS:
                        weigh(h + 1)
                    if h + 2 < HEADS - 1:
                        low(u0 + 2 * KD + h + 6)
                    dve.wait_ge(s_dsq, h + 1)
                    dve.wait_ge(s_ms, h + 1)
                    nc.vector.scalar_tensor_tensor(out=den[:, s, :], in0=psum[:, 7, :], scalar=1 / P,
                                                   in1=den[:, s, :], op0=ALU.mult, op1=ALU.add).then_inc(s_tt, 1)
                    dve.wait_ge(s_sdm, h + 1)
                    nc.vector.reciprocal(den[:, s, :], den[:, s, :]).then_inc(s_rr, 1)
                    dve.wait_ge(s_rr, h + 1)
                    nc.vector.tensor_tensor(y_of(h), psum[:, 3 + s, :], den[:, s, :], ALU.mult).then_inc(s_y1, 1)

                def gate(h):
                    dve.wait_ge(s_y1, h + 1)
                    dve.wait_ge(s_og, h + 1)
                    nc.vector.scalar_tensor_tensor(out=y_of(h), in0=y_of(h), scalar=cols[:, 0, 104 + h:105 + h],
                                                   in1=sig[:, h, :], op0=ALU.mult, op1=ALU.mult).then_inc(s_y2, 1)

                gate(0)
                for h in range(HEADS):
                    if h + 1 < HEADS:
                        gate(h + 1)
                    dve.wait_ge(s_y2, h + 1)
                    dve.wait_ge(s_yh, h + 1)
                    nc.vector.tensor_tensor(xl[:, h, :], y_of(h), xh[:, h, :].bitcast(F32),
                                            ALU.subtract).then_inc(s_yr, 1)
                    if h == 1:
                        low(u0 + 3 * KD + 3)
                for d in range(d0(n)):
                    low(u0 + 3 * KD + 4 + d)
                    z_tile(n, d, d, u0 + 3 * KD + d)
                layer_norm(n)

            def attention():
                n = 4
                dve.wait_ge(s_x, 2 * (n + 1) * KD)

                def head(t, prev):
                    for j in range(9):
                        m = t * 9 + j
                        low(m + (ATT0 + ATT_RING))
                        if prev is not None:
                            if j == 0:
                                v_tokens(prev, 2)
                            if j == 1:
                                token_stats(prev)
                            if j == 3:
                                scale_prob(prev)
                            if j == 4:
                                prob_out(prev)
                            if j == 5:
                                out_join(prev)
                            if j == 6:
                                out_low(prev)
                        if j == 6:
                            mask_scores(t)
                        if j == 7:
                            v_tokens(t, 0)
                        if j == 8:
                            v_tokens(t, 1)
                            class_stats(t)

                def v_tokens(t, g):
                    wait(dve, s_vt, t * 3 + (START + KD + g + 1))
                    nc.vector.tensor_copy(vt[:, g, :, :], psum[:, 7, :].rearrange("p (b q) -> p b q", q=P)
                                          ).then_inc(s_vc, 1)

                def mask_scores(t):
                    wait(dve, s_as, t + 1)
                    own = lambda n_b: mask[:, 1:2, :].broadcast_to([P, n_b, P])

                    def masked(lo, n_b, bank, col, m):
                        nc.vector.tensor_tensor(prob[:, lo:lo + n_b, :],
                                                psum[:, bank, col * P:(col + n_b) * P].rearrange(
                                                    "p (b q) -> p b q", q=P), m, ALU.add).then_inc(s_am, 1)

                    masked(0, 1, 3, 0, own(1))
                    masked(1, 2, 3, 1, mask[:, 0:2, :])
                    masked(3, 2, 4, 0, mask[:, 0:2, :])
                    masked(5, 2, 4, 2, mask[:, 0:2, :])
                    masked(7, 4, 5, 0, own(4))
                    masked(11, 4, 6, 0, mask[:, 2:3, :].broadcast_to([P, 4, P]))
                    wait(dve, s_am, t * 6 + 6)
                    nc.vector.tensor_reduce(mx[:, 0, 0:1], prob[:, 0, :], AX.X, ALU.max).then_inc(s_mxr, 1)
                    nc.vector.tensor_reduce(mx[:, 0, 1:4], prob[:, 1:7, :].rearrange("p (b c) q -> p b (c q)", c=2),
                                            AX.X, ALU.max).then_inc(s_mxr, 1)
                    nc.vector.tensor_reduce(mx[:, 1:3, :].rearrange("p g b -> p (g b)"), prob[:, 7:15, :],
                                            AX.X, ALU.max).then_inc(s_mxr, 1)
                    wait(dve, s_mxr, t * 3 + 3)
                    nc.vector.tensor_scalar(nb[:, :, :], mx[:, :, :], -SCALE, None, ALU.mult).then_inc(s_nb, 1)

                def class_stats(t):
                    nc.vector.tensor_tensor(pm[:, 0, :], mx[:, 1, :], mx[:, 2, :], ALU.max).then_inc(s_pc, 1)
                    wait(dve, s_pc, t * 6 + 1)
                    for g in range(2):
                        nc.vector.tensor_tensor(pd[:, g, :], mx[:, 1 + g, :], pm[:, 0, :], ALU.subtract
                                                ).then_inc(s_pc, 1)
                    wait(dve, s_pe, t + 1)
                    wait(dve, s_ae, t * 12 + 12)
                    for g in range(2):
                        nc.vector.tensor_tensor(pd[:, g, :], pe12[:, g, :], dn[:, 1 + g, :], ALU.mult
                                                ).then_inc(s_pc, 1)
                    wait(dve, s_pc, t * 6 + 5)
                    nc.vector.tensor_tensor(pm[:, 1, :], pd[:, 0, :], pd[:, 1, :], ALU.add).then_inc(s_pc, 1)

                def token_stats(t):
                    wait(dve, s_pld, t * 16 + 16)
                    nc.vector.tensor_tensor(nd[:, 0, :], mx[:, 0, :], nm[:, 0, :], ALU.max).then_inc(s_nc, 1)
                    wait(dve, s_nc, t * 8 + 1)
                    nc.vector.tensor_tensor(nj[:, 0, :], mx[:, 0, :], nd[:, 0, :], ALU.subtract).then_inc(s_nc, 1)
                    nc.vector.tensor_tensor(nj[:, 1, :], nm[:, 0, :], nd[:, 0, :], ALU.subtract).then_inc(s_nc, 1)
                    wait(dve, s_ne, t + 1)
                    nc.vector.tensor_tensor(nd[:, 0, :], dn[:, 0, :], ne[:, 0, :], ALU.mult).then_inc(s_nc, 1)
                    nc.vector.tensor_tensor(nd[:, 1, :], nm[:, 1, :], ne[:, 1, :], ALU.mult).then_inc(s_nc, 1)
                    wait(dve, s_nc, t * 8 + 5)
                    nc.vector.tensor_tensor(nd[:, 0, :], nd[:, 0, :], nd[:, 1, :], ALU.add).then_inc(s_nc, 1)
                    wait(dve, s_nc, t * 8 + 6)
                    nc.vector.reciprocal(nd[:, 1, :], nd[:, 0, :]).then_inc(s_nc, 1)
                    wait(dve, s_nc, t * 8 + 7)
                    nc.vector.tensor_tensor(f12[:, :], ne[:, 1, :], nd[:, 1, :], ALU.mult).then_inc(s_nc, 1)
                    nc.vector.tensor_tensor(fac[:, 0, :], ne[:, 0, :], nd[:, 1, :], ALU.mult).then_inc(s_fac, 1)

                def scale_prob(t):
                    wait(dve, s_nld, t * 16 + 16)
                    for g in range(2):
                        nc.vector.tensor_tensor(fac[:, 1 + g, :], pe12[:, g, :], pf[:, :], ALU.mult
                                                ).then_inc(s_fac, 1)
                    wait(dve, s_fac, t * 3 + 3)

                    def scaled(blk, f, shape):
                        nc.vector.tensor_tensor(blk, blk, f.unsqueeze(2).broadcast_to(shape), ALU.mult
                                                ).then_inc(s_sc, 1)

                    scaled(prob[:, 0:1, :], fac[:, 0, 0:1], [P, 1, P])
                    scaled(prob[:, 1:7, :].rearrange("p (b c) q -> p b (c q)", c=2), fac[:, 0, 1:4], [P, 3, 2 * P])
                    scaled(prob[:, 7:15, :], fac[:, 1:3, :].rearrange("p g b -> p (g b)"), [P, 8, P])

                def prob_out(t):
                    wait(dve, s_pt, t + 1)
                    nc.vector.tensor_copy(probT[:, 4:8, :].rearrange("p b q -> p (b q)"), psum[:, 4, :]).then_inc(s_ptd, 1)
                    nc.vector.tensor_copy(probT[:, 12:15, :].rearrange("p b q -> p (b q)"), psum[:, 6, 0:3 * P]
                                          ).then_inc(s_ptd, 1)

                def out_join(t):
                    wait(dve, s_on, t + 1)
                    y = yn[:, :].rearrange("p (i r) -> p i r", r=DIL)
                    nc.vector.tensor_tensor(y, y, psum[:, 3, :].rearrange("p (r i) -> p i r", r=DIL), ALU.add
                                            ).then_inc(s_oe, 1)

                def out_low(t):
                    wait(dve, s_yh, t + (HEADS + 1))
                    nc.vector.tensor_tensor(yl[:, one(t), :], yn[:, :].unsqueeze(1),
                                            yh[:, one(t), :].bitcast(F32), ALU.subtract).then_inc(s_yr, 1)

                head(Pos(0), None)
                with dve.Fori(0, HEADS - 1) as i:
                    head(Pos(1, 1, i), Pos(0, 1, i))
                t = Pos(HEADS - 1)
                v_tokens(t, 2)
                derive(n, 1.0)
                low(ATT1 + ATT_RING)
                token_stats(t)
                clear_sums(n)
                scale_prob(t)
                prob_out(t)
                out_join(t)
                out_low(t)
                for d in range(d0(n)):
                    low(ATT1 + 4 + d)
                    z_tile(n, d, d, ATT1 + d)
                layer_norm(n)

            for k, (s, count) in enumerate(((s_z, START), (s_gu, START), (s_hl, START), (s_ev, EV_START), (s_cf, START),
                             (s_vt, START), (s_vc, START), (s_qk, START))):
                nc.vector.memset(token[:, k:k + 1], 0.0).then_inc(s, count)
            dve.wait_ge(s_colsT, 1)
            nc.vector.tensor_copy(cols[:, 0, 0:112], psum[:, 4, 0:112]).then_inc(s_cols, 1)
            dve.wait_ge(s_colsT, 3)
            nc.vector.tensor_copy(cols[:, 1, 0:104], psum[:, 5, 0:104]).then_inc(s_cols, 1)
            nc.vector.tensor_copy(cols[:, 2, 0:72], psum[:, 6, 0:72]).then_inc(s_cols, 1)
            dve.wait_ge(s_const, 7)
            nc.vector.tensor_reduce(sel4[:, :], ident[:, :].rearrange("p (a b) -> p b a", b=DIL), AX.X, ALU.add
                                    ).then_inc(s_mask, 1)
            dve.wait_ge(s_mask, 1)
            nc.vector.tensor_scalar(sel4[:, :], sel4[:, :], -MASKED, MASKED, ALU.mult, ALU.add).then_inc(s_mask, 1)
            dve.wait_ge(s_mask, 2)
            nc.vector.tensor_tensor(mask[:, 2, :].rearrange("p (a b) -> p a b", b=DIL),
                                    mask[:, 1, :].rearrange("p (a b) -> p a b", b=DIL),
                                    sel4[:, :].unsqueeze(1).broadcast_to([P, P // DIL, DIL]), ALU.add
                                    ).then_inc(s_mask, 1)
            dve.wait_ge(s_cond, 1)

            def first_macs(a, ks):
                total = ada_first[:, a, 0, :]
                for k in ks:
                    dve.wait_ge(s_first[a][k], 16)
                    if k == 0:
                        nc.vector.tensor_scalar(total, total, cond[:, 0:1], None, ALU.mult).then_inc(s_ada, 2)
                    else:
                        dve.wait_ge(s_ada, 2 * (KD * a + k))
                        nc.vector.scalar_tensor_tensor(out=total, in0=ada_first[:, a, k, :], scalar=cond[:, k:k + 1],
                                                       in1=total, op0=ALU.mult, op1=ALU.add).then_inc(s_ada, 2)

            def first_factors(a):
                part = lambda v: v.rearrange("p (s t) -> p s t", s=2)[:, :, 4 * a:4 * a + 4]
                t = slice(4 * a, 4 * a + 4)
                dve.wait_ge(s_modp, 2 * (a + 1))
                nc.vector.tensor_tensor(part(mod[:, 0:2 * KD]), part(psum[:, 7, 0:2 * KD]),
                                        part(cols[:, 1, 0:2 * KD]), ALU.add).then_inc(s_mod, 2)
                dve.wait_ge(s_mod, 2 * (a + 1))
                nc.vector.tensor_scalar(mul_c[:, t], mod[:, KD + 4 * a:KD + 4 * a + 4], 1.0, None, ALU.add
                                        ).then_inc(s_der, 1)
                nc.vector.tensor_copy(add_c[:, t], mod[:, t]).then_inc(s_der, 1)
                dve.wait_ge(s_der, 2 * (a + 1))

            def first_low(a):
                half, d = FIRST_TILES[a]
                dve.wait_ge(s_xnew, d + 1)
                if a >= 2:
                    dve.wait_ge(s_x, a - 1)
                nc.vector.tensor_scalar(ln_m[:, a % 2, :], xres[:, d, cols_of(half)], mul_c[:, d:d + 1],
                                        add_c[:, d:d + 1], ALU.mult, ALU.add).then_inc(s_xm, 1)
                dve.wait_ge(s_xm, a + 1)
                dve.wait_ge(s_xhi, a + 1)
                nc.vector.tensor_tensor(xl[:, d, cols_of(half)], ln_m[:, a % 2, :],
                                        xh[:, d, cols_of(half)].bitcast(F32), ALU.subtract).then_inc(s_x, 1)

            first_macs(0, range(KD))
            low(0)
            low(1)
            first_factors(0)
            for a in range(2):
                first_low(a)
            low(2)
            for a in (2, 3):
                first_low(a)
            low(3)
            for a in range(4, KD):
                first_low(a)
            first_macs(1, range(KD))
            first_factors(1)
            for a in range(KD, 2 * KD):
                first_low(a)
            ffn(0)
            mlstm()
            ffn(2)
            ffn(3)
            attention()
            ffn(5)
            for b in range(NB):
                dve.wait_ge(s_fT, 2 * b + 2)
                nc.vector.tensor_copy(xtok[:, b, SEQ:], psum[:, 2 * b + 1, :]).then_inc(s_fo2, 1)

        @block.tensor
        def _(pe):
            def products(u, k, out_ap, rh, rl, start, stop):
                s = slot_of(u)
                for w, r, first, last in ((w_hi, rh, True, False), (w_hi, rl, False, False), (w_lo, rh, False, True)):
                    mm = nc.tensor.matmul(out_ap, w[:, s, k, :], r, start=start and first, stop=stop and last)
                return mm

            def strip(u, bank, kts=KD, rh=xh, rl=xl, k0=0, start=True, stop=True):
                wait(pe, s_lo, pos(u) + 1)
                for k in range(kts):
                    mm = products(u, k, psum[:, bank, :], rh[:, k0 + k, :], rl[:, k0 + k, :],
                                  start and k == 0, stop and k == kts - 1)
                mm.then_inc(s_unit, 1)

            def first_strips_of_all():
                for k in range(KD):
                    if k == KD // 2:
                        first_sums(1)
                    pe.wait_ge(s_x, 2 * k + 2)
                    for j in range(RING):
                        if k < JOIN[j]:
                            continue
                        if k == JOIN[j]:
                            pe.wait_ge(s_lo, j + 1)
                        for kk in range(k + 1) if k == JOIN[j] else (k,):
                            mm = products(j, kk, psum[:, j, :], xh[:, kk, :], xl[:, kk, :], kk == 0, kk == KD - 1)
                        if k == KD - 1:
                            mm.then_inc(s_unit, 1)

            def first_sums(a):
                pe.wait_ge(s_ada, 2 * KD * (a + 1))
                if a:
                    pe.wait_ge(s_mod, 2)
                for j in range(KD):
                    col = (j // 4) * KD + 4 * a + j % 4
                    mm = nc.tensor.matmul(psum[:, 7, col:col + 1], ada_first[:, a, 0, j * P:(j + 1) * P],
                                          ones[:, 0:1], start=True, stop=True)
                mm.then_inc(s_modp, 2)

            def first_strips(n, count):
                for half in range(2):
                    c = cols_of(half)
                    for k in range(KD):
                        pe.wait_ge(s_x, 2 * KD * n + KD * half + k + 1)
                        for j in range(count):
                            joins = half == 0 and k == JOIN[j]
                            if half == 0 and k < JOIN[j]:
                                continue
                            if joins:
                                pe.wait_ge(s_lo, FIRST[n] + j + 1)
                            for kk in range(k + 1) if joins else (k,):
                                mm = products(FIRST[n] + j, kk, psum[:, j, c], xh[:, kk, c], xl[:, kk, c],
                                              kk == 0, kk == KD - 1)
                            if half and k == KD - 1:
                                mm.then_inc(s_unit, 1)
                        if half == 0 and n > 0:
                            if k == 1:
                                sums(n - 1, 1)
                            if k == 3:
                                spread(n - 1, 1)

            def halves(n, first_unit, rh, rl):
                units = [(i, q) for i in range(tail(n)) for q in range(tail_units(n) // tail(n))]
                per = len(units) // tail(n)
                for half in range(2):
                    c = cols_of(half)
                    for a, (i, q) in enumerate(units):
                        k0, kt = K_CHUNKS[q] if n in ffn_index else (0, KD)
                        bank = tail_bank(n, half, i)
                        if half == 0:
                            pe.wait_ge(s_lo, first_unit + a + 1)
                        if q == 0:
                            read = d0(n) + i - 1 if half == 0 else d0(n) + (0 if n in ffn_index else i + 1)
                            pe.wait_ge(s_z, z_before(n) + read)
                        for k in range(kt):
                            if half and len(units) == 2 and a == 1 and k == 4:
                                spread(n, 0)
                            mm = products(first_unit + a, k, psum[:, bank, c], rh[:, k0 + k, c], rl[:, k0 + k, c],
                                          q == 0 and k == 0, q == per - 1 and k == kt - 1)
                        if half:
                            mm.then_inc(s_unit, 1)
                        elif q == per - 1:
                            mm.then_inc(s_tail, 1)
                        if half and a == 0:
                            sums(n, 0)
                        if half and a == 1 and len(units) == 3:
                            spread(n, 0)
                    if half == 0 and n == 0:
                        mod_sum(ada_chunks(n) + NF // 2 + 2)

            def mod_sum(ch):
                wait(pe, s_ada, pos(ch) * KD + KD)
                for j in range(4):
                    mm = nc.tensor.matmul(psum[:, 7, j:j + 1], ada_acc[:, j * P:(j + 1) * P], ones[:, 0:1],
                                          start=True, stop=True)
                mm.then_inc(s_modp, 1)

            def sums(n, half):
                done = acc_before(n) + 1 + d0(n) + (tail(n) - 1) * (half + 1)
                pe.wait_ge(s_acc1, done)
                pe.wait_ge(s_acc2, done)
                pe.wait_ge(s_z, z_before(n) + d0(n) + tail(n) * (half + 1))
                pe.wait_ge(s_sq, sq_before(n) + d0(n) + tail(n) * (half + 1))
                if half and ada_rounds(n):
                    pe.wait_ge(s_mod, ada_chunks(n + 1))
                for a, last in ((0, xres[:, KD - 1, :]), (1, sq)):
                    for b in range(2):
                        t = slice((2 * half + b) * P, (2 * half + b + 1) * P)
                        dst = psum[:, 6 + half, 2 * a + b:2 * a + b + 1]
                        nc.tensor.matmul(dst, acc[:, a, t], ones[:, 0:1], start=True, stop=False)
                        mm = nc.tensor.matmul(dst, last[:, t], ones[:, 0:1], start=False, stop=True)
                mm.then_inc(s_stat, 1)

            def spread(n, half):
                pe.wait_ge(s_rstd, 2 * n + half + 1)
                for a, q in enumerate((0, 4)):
                    for b in range(2):
                        mm = nc.tensor.matmul(psum[:, 6 + half, (2 * a + b) * P:(2 * a + b + 1) * P],
                                              st[:, half, q, b:b + 1].broadcast_to([P, P]), ident[:, :],
                                              start=True, stop=True)
                mm.then_inc(s_bc, 1)

            def ffn(n):
                u0, h0, c0 = FIRST[n], START + NF * ffn_index[n], ada_chunks(n)
                pe.wait_ge(s_gu, h0)
                if n == 0:
                    first_strips_of_all()
                else:
                    first_strips(n, RING)

                def in_round(i, start, with_ada):
                    for j in range(2):
                        wait(pe, s_gu, Pos(h0 + 2 * start + j + 1, 2, i))
                        strip(Pos(u0 + 4 * start + 4 + 2 * j, 4, i), 2 * j)
                        strip(Pos(u0 + 4 * start + 5 + 2 * j, 4, i), 2 * j + 1)
                        if with_ada and j == 0:
                            mod_sum(Pos(c0 + start, 1, i))

                r = min(ada_rounds(n), NF // 2 - 1)
                if r:
                    with pe.Fori(0, r) as i:
                        in_round(i, 0, True)
                if r < NF // 2 - 1:
                    with pe.Fori(0, NF // 2 - 1 - r) as i:
                        in_round(i, r, False)
                for d in range(d0(n)):
                    pe.wait_ge(s_z, z_before(n) + d - 1)
                    for q, (k0, kt) in enumerate(K_CHUNKS):
                        if d == 0:
                            pe.wait_ge(s_hl, h0 + k0 + kt)
                        strip(u0 + 2 * NF + 3 * d + q, 4 + d % 2, kt, hh, hl, k0, q == 0, q == 2)
                    if d == 0 and ada_rounds(n) == NF // 2:
                        mod_sum(c0 + NF // 2 - 1)
                    if n == 0 and d in (1, 4):
                        mod_sum(c0 + NF // 2 + d // 4)
                halves(n, u0 + 2 * NF + 3 * d0(n), hh, hl)

            def mlstm():
                n, u0, e0 = 1, FIRST[1], ev_before(1)
                first_strips(n, RING)
                def gate_products():
                    pe.wait_ge(s_glo, 1)
                    for k in range(KD):
                        for w, r, first, last in ((g_hi, xh, k == 0, False), (g_hi, xl, False, False),
                                                  (g_lo, xh, False, k == KD - 1)):
                            mm = nc.tensor.matmul(psum[:, 6, :], w[:, k, :], r[:, k, :], start=first, stop=last)
                    mm.then_inc(s_gp, 1)

                for j in range(4):
                    pe.wait_ge(s_ev, e0 + j + 1)
                    strip(u0 + 4 + j, j)
                    if j == 0:
                        gate_products()
                with pe.Fori(0, 2) as i:
                    def turn(j):
                        h = Pos(j, 4, i)
                        wait(pe, s_ev, h + (e0 + KD + 1))
                        wait(pe, s_vc, h + (START - 1))
                        for b in range(NB):
                            mm = nc.tensor.transpose(psum[:, 4 + j % 2, b * P:(b + 1) * P],
                                                     duo[:, j % 2, b * P:(b + 1) * P], ident[:, :])
                        mm.then_inc(s_vt, 1)
                    for j in range(4):
                        m = Pos(KD + j, 4, i)
                        wait(pe, s_ev, m + (e0 - 3))
                        strip(m + u0, j)
                        if j >= 1:
                            turn(j - 1)
                    turn(3)

                pe.wait_ge(s_gr, 7 + 2 * NB)
                for b in range(NB):
                    mm = nc.tensor.transpose(psum[:, 7, b * HEADS:(b + 1) * HEADS],
                                             grow[:, 6, b * P:(b + 1) * P], ident[0:HEADS, 0:HEADS])
                mm.then_inc(s_cT, 1)

                def gate_strip(h):
                    if h:
                        pe.wait_ge(s_ev, e0 + 2 * KD + h)
                    strip(u0 + 2 * KD + h, 6)

                def scores(h):
                    a, o = h // 2, DQK * (h % 2)
                    if h >= 1:
                        pe.wait_ge(s_SD, 3 * h)
                    for b in range(NB):
                        bank, col = ((0, 0), (1, 0), (2, 0), (2, 2 * P))[b]
                        mm = nc.tensor.matmul(psum[:, bank, col:col + SEQ - b * P],
                                              qk[o:o + DQK, HEADS // 2 + a, b * P:(b + 1) * P],
                                              qk[o:o + DQK, a, b * P:], start=True, stop=True)
                    mm.then_inc(s_S, 1)

                pe.wait_ge(s_qk, START + KD)
                pe.wait_ge(s_vc, START + KD)
                gate_strip(0)
                scores(0)
                gate_strip(1)
                for h in range(HEADS):
                    s = h % 2
                    pe.wait_ge(s_SD, 3 * (h + 1))
                    if h >= 2:
                        pe.wait_ge(s_y1, h - 1)
                    for b in range(NB):
                        nc.tensor.matmul(psum[:, 3 + s, b * P:], vtok[:, b, h * P:(h + 1) * P],
                                         dmat[:, s, SEG[b]:SEG[b + 1]], start=(b == 0), stop=(b == NB - 1))
                    if h >= 1:
                        pe.wait_ge(s_ab, h)
                    for b in range(NB):
                        mm = nc.tensor.matmul(psum[:, 5, b * P:], ones[:, :], dmat[:, s, SEG[b]:SEG[b + 1]],
                                              start=(b == 0), stop=(b == NB - 1))
                    mm.then_inc(s_nd, 1)
                    if h + 1 < HEADS:
                        scores(h + 1)
                    if h + 2 < HEADS - 1:
                        gate_strip(h + 2)
                    pe.wait_ge(s_nsq, h + 1)
                    if h >= 1:
                        pe.wait_ge(s_tt, h)
                    nc.tensor.matmul(psum[:, 7, :], ones[:, :], nsq[:, :], start=True, stop=True).then_inc(s_ms, 1)
                gate_strip(HEADS - 1)
                pe.wait_ge(s_y1, HEADS)
                def head_tile(d, k):
                    mm = products(u0 + 3 * KD + d, k, psum[:, d, :], xh[:, k, :], xl[:, k, :], k == 0, k == HEADS - 1)
                    if k == HEADS - 1:
                        mm.then_inc(s_unit, 1)

                for k in range(HEADS // 2):
                    pe.wait_ge(s_yr, k + 1)
                    for d in range(3):
                        if k == 0:
                            pe.wait_ge(s_lo, u0 + 3 * KD + d + 1)
                        head_tile(d, k)
                    if k >= 2:
                        pe.wait_ge(s_lo, u0 + 3 * KD + 4)
                        for kk in range(3) if k == 2 else (k,):
                            head_tile(3, kk)
                for d in range(4):
                    for k in range(HEADS // 2, HEADS):
                        pe.wait_ge(s_yr, k + 1)
                        head_tile(d, k)
                for d in range(4, d0(n)):
                    strip(u0 + 3 * KD + d, d)
                halves(n, u0 + 3 * KD + d0(n), xh, xl)

            def attention():
                n, e0 = 4, ev_before(4)

                def head(t, prev):
                    for j in range(9):
                        m = t * 9 + j
                        if prev is not None or j >= ATT_RING:
                            wait(pe, s_ev, m + (e0 - 2))
                            strip(m + ATT0, j % 3)
                        if prev is not None:
                            if j == 0:
                                turn(prev, 2)
                            if j == 4:
                                prob_turn(prev)
                            if j == 5:
                                values(prev)
                        if j == 6:
                            scores(t)
                        if j == 7:
                            turn(t, 0)
                        if j == 8:
                            turn(t, 1)

                def turn(t, g):
                    wait(pe, s_ev, t * 9 + (e0 + 7 + g))
                    wait(pe, s_vc, t * 3 + (START + KD + g))
                    if g == 0:
                        wait(pe, s_on, t)
                    for b in range(NB):
                        mm = nc.tensor.transpose(psum[:, 7, b * P:(b + 1) * P], duo[:, g % 2, b * P:(b + 1) * P],
                                                 ident[:, :])
                    mm.then_inc(s_vt, 1)

                def scores(t):
                    wait(pe, s_ev, t * 9 + (e0 + 6))
                    wait(pe, s_oe, t)
                    for b in range(NB):
                        lo = max(b - 1, 0)
                        bank, col = ((3, 0), (3, 1), (4, 0), (4, 2))[b]
                        nc.tensor.matmul(psum[:, bank, col * P:(col + b + 1 - lo) * P],
                                         qT[:, 0, b * P:(b + 1) * P], kT[:, 0, lo * P:(b + 1) * P],
                                         start=True, stop=True)
                    for g in (1, 2):
                        for b in range(NB):
                            mm = nc.tensor.matmul(psum[:, 4 + g, b * P:(b + 1) * P], qT[:, g, b * P:(b + 1) * P],
                                                  kT[:, g, b * P:(b + 1) * P], start=True, stop=True)
                    mm.then_inc(s_as, 1)

                def prob_turn(t):
                    wait(pe, s_sc, t * 3 + 3)
                    for b in range(ATT_BLOCKS):
                        mm = nc.tensor.transpose(psum[:, 3 + b // 4, (b % 4) * P:(b % 4 + 1) * P], prob[:, b, :],
                                                 ident[:, :])
                    mm.then_inc(s_pt, 1)

                def values(t):
                    wait(pe, s_pta, t * 2 + 2)
                    wait(pe, s_ptd, t * 2 + 2)
                    wait(pe, s_vc, t * 3 + (START + KD + 3))
                    for b in range(NB):
                        dst = psum[:, 7, b * P:(b + 1) * P]
                        if b:
                            nc.tensor.matmul(dst, vt[:, 0, b - 1, :], probT[:, 2 * b - 1, :], start=True, stop=False)
                        nc.tensor.matmul(dst, vt[:, 0, b, :], probT[:, 2 * b, :], start=(b == 0), stop=True)
                    for b in range(NB):
                        dst = psum[:, 3, b * P:(b + 1) * P]
                        nc.tensor.matmul(dst, vt[:, 1, b, :], probT[:, 7 + b, :], start=True, stop=False)
                        mm = nc.tensor.matmul(dst, vt[:, 2, b, :], probT[:, 11 + b, :], start=False, stop=True)
                    mm.then_inc(s_o, 1)

                first_strips(n, ATT_RING)
                head(Pos(0), None)
                with pe.Fori(0, HEADS - 1) as i:
                    head(Pos(1, 1, i), Pos(0, 1, i))
                t = Pos(HEADS - 1)
                turn(t, 2)
                pe.wait_ge(s_ev, e0 + ATT_HEAD_UNITS)
                pe.wait_ge(s_lo, ATT1 + 3)
                for k in range(HEADS - 1):
                    pe.wait_ge(s_yr, HEADS + k + 1)
                    for d in range(3):
                        products(ATT1 + d, k, psum[:, d, :], yh[:, k, :], yl[:, k, :], k == 0, False)
                prob_turn(t)
                values(t)
                pe.wait_ge(s_yr, 2 * HEADS)
                for d in range(3):
                    products(ATT1 + d, HEADS - 1, psum[:, d, :], yh[:, HEADS - 1, :], yl[:, HEADS - 1, :],
                             False, True).then_inc(s_unit, 1)
                for d in range(3, d0(n)):
                    strip(ATT1 + d, d, KD, yh, yl)
                halves(n, ATT1 + d0(n), yh, yl)

            pe.wait_ge(s_const, 5)
            pe.wait_ge(s_rows[0], 16 * 4)
            for a, rows in enumerate((112, 104, 72)):
                if a == 1:
                    pe.wait_ge(s_rows[1], 16 * 3)
                nc.tensor.transpose(psum[:, 4 + a, 0:rows], rows_t[0:rows, a, :], ident[0:rows, 0:rows]
                                    ).then_inc(s_colsT, 1)
            pe.wait_ge(s_xtok, 16)
            for d in range(KD):
                if d >= 4:
                    pe.wait_ge(s_xnew, d - 3)
                for b in range(NB):
                    mm = nc.tensor.transpose(psum[:, d % 4, b * P:(b + 1) * P], xtok[:, b, d * P:(d + 1) * P],
                                             ident[:, :])
                mm.then_inc(s_xT, 1)
            first_sums(0)
            ffn(0)
            mlstm()
            ffn(2)
            ffn(3)
            attention()
            ffn(5)
            sums(NLAYERS - 1, 1)
            spread(NLAYERS - 1, 1)
            for b in range(NB):
                pe.wait_ge(s_xnew, xnew_before(NLAYERS) - (KD if b < NB // 2 else 0))
                for d in range(KD):
                    mm = nc.tensor.transpose(psum[:, 2 * b + d // 4, (d % 4) * P:(d % 4 + 1) * P],
                                             xres[:, d, b * P:(b + 1) * P], ident[:, :])
                    if d % 4 == 3:
                        mm.then_inc(s_fT, 1)


GATE_ROW_STEPS = 7 + 3 * NB

_INS = ['x', 'c', 'ada_w', 'ada_b', 'ln_g', 'ln_b', 'ffn_w_in', 'ffn_w_out', 'mlstm_w_in', 'mlstm_gate_bias',
        'mlstm_conv_w', 'mlstm_head_gain', 'mlstm_w_out', 'attn_w_in', 'attn_w_out']


def kernel(**inputs):
    import numpy as _np
    import concourse.bacc as _bacc
    from concourse import mybir as _mybir
    from concourse.bass_utils import run_bass_kernel_spmd as _run

    nc = _bacc.Bacc("TRN2", target_bir_lowering=False, num_devices=1)
    arrays, args = {}, []
    for name in _INS:
        a = _np.ascontiguousarray(inputs[name])
        arrays[f"in_{name}"] = a
        args.append(nc.dram_tensor(f"in_{name}", a.shape, _mybir.dt.from_np(a.dtype), kind="ExternalInput").ap())
    args.append(nc.dram_tensor("out_0", (1, SEQ, D_MODEL), F32, kind="ExternalOutput").ap())
    trunk(nc, *args)
    r = _run(nc, [arrays], core_ids=[0])
    return r.results[0]["out_0"]
```
